# Optimizing a Trainium2 kernel written in Bass

```python
import jax, jax.numpy as jnp
from jax import lax
import numpy as np

D_MODEL = 2048
BATCH = 1
SEQ = 256
DEPTH = 2

CHUNK = 64
MEM_LEN = 256
HEAD_DIM = 128
MIX_WIDTH = D_MODEL
HALF_WIDTH = MIX_WIDTH // 2
POOL_GROUPS = 4
POOL_WINDOWS = (2, 4, 8, 16)
POOL_GROUP_DIM = HALF_WIDTH // POOL_GROUPS
DSA_HEADS = HALF_WIDTH // HEAD_DIM
IDX_HEADS = 16
IDX_DIM = 64
DSA_TOPK_MAX = 256
DSA_BLOCK = 64
CONV_WIDTH = 3
CONV_DIM = HALF_WIDTH
FOX_HEADS = HALF_WIDTH // HEAD_DIM
FOX_BLOCK = 128
FORGET_BIAS_INIT = 2.0
XA_HEADS = 4
XA_WIDTH = XA_HEADS * HEAD_DIM
FFN_HIDDEN = -(-(8 * D_MODEL) // (3 * 256)) * 256
ROPE_THETA = 500000.0
ROPE_FRACTION = 4
LN_EPS = 1e-5
ALPHA = (2 * DEPTH) ** 0.25
BETA = (8 * DEPTH) ** -0.25
N_EVEN = (DEPTH + 1) // 2
N_ODD = DEPTH // 2
EV_SIZES = (HALF_WIDTH, HALF_WIDTH, HALF_WIDTH, HALF_WIDTH, IDX_HEADS * IDX_DIM, IDX_DIM, IDX_HEADS)
EV_IN = sum(EV_SIZES)
OD_SIZES = (CONV_DIM, CONV_DIM, CONV_DIM, HALF_WIDTH, HALF_WIDTH, HALF_WIDTH, FOX_HEADS)
OD_IN = sum(OD_SIZES)

kernel_name = "hybrid_pool_dsa_conv_fox_deepnorm_trunk"

def split_cols(h, sizes):
    offs, acc = [], 0
    for s in sizes[:-1]:
        acc += s
        offs.append(acc)
    return jnp.split(h, offs, axis=-1)

def layer_norm(x, g, b):
    xf = x.astype(jnp.float32)
    mu = jnp.mean(xf, axis=-1, keepdims=True)
    var = jnp.mean(jnp.square(xf - mu), axis=-1, keepdims=True)
    return ((xf - mu) * lax.rsqrt(var + LN_EPS) * g + b).astype(x.dtype)

def partial_rotary(x, positions):
    dh = x.shape[-1]
    rot = dh // ROPE_FRACTION
    half = rot // 2
    inv_freq = jnp.power(ROPE_THETA, -(jnp.arange(half, dtype=jnp.float32) * 2.0 / rot))
    ang = positions.astype(jnp.float32)[..., None] * inv_freq
    cos = jnp.cos(ang)[:, :, None, :]
    sin = jnp.sin(ang)[:, :, None, :]
    x1 = x[..., :half].astype(jnp.float32)
    x2 = x[..., half:rot].astype(jnp.float32)
    xr = jnp.concatenate([x1 * cos - x2 * sin, x2 * cos + x1 * sin], axis=-1).astype(x.dtype)
    return jnp.concatenate([xr, x[..., rot:]], axis=-1)

def pool_mixer(u, w_groups, scale):
    B, S, C = u.shape
    uf = u.astype(jnp.float32)
    cs = jnp.cumsum(uf, axis=1)
    cnt = jnp.arange(1, S + 1, dtype=jnp.float32)[None, :, None]
    ug = jnp.split(uf, POOL_GROUPS, axis=-1)
    cg = jnp.split(cs, POOL_GROUPS, axis=-1)
    outs = []
    for w, u_g, c_g in zip(POOL_WINDOWS, ug, cg):
        lag = jnp.pad(c_g, ((0, 0), (w, 0), (0, 0)))[:, :S]
        outs.append((c_g - lag) / jnp.minimum(cnt, float(w)) - u_g)
    d = jnp.stack(outs, axis=2).astype(u.dtype)
    y = jnp.einsum('bsgc,gcd->bsgd', d, w_groups)
    return y.reshape(B, S, C) * scale

def dsa_attention(q, k, v, qi, ki, wi):
    B, S, H, Dh = q.shape
    topk = min(DSA_TOPK_MAX, S // 4)
    nblk = S // DSA_BLOCK
    s_idx = jnp.arange(S, dtype=jnp.int32)
    scale = Dh ** -0.5
    gather = jax.vmap(lambda a, i: a[i])

    def block(args):
        qb, qib, wib, t0 = args
        t = t0 + jnp.arange(DSA_BLOCK, dtype=jnp.int32)
        il = jnp.einsum('bthd,bsd->bths', qib, ki) * (IDX_DIM ** -0.5)
        score = jnp.einsum('bths,bth->bts', jax.nn.relu(il), wib).astype(jnp.float32)
        admissible = (s_idx[None, :] // CHUNK) <= (t[:, None] // CHUNK)
        score = jnp.where(admissible[None], score, -jnp.inf)
        _, idx = lax.top_k(score, topk)
        valid = (idx // CHUNK) <= (t // CHUNK)[None, :, None]
        ks = gather(k, idx)
        vs = gather(v, idx)
        logits = jnp.einsum('bthd,btkhd->bthk', qb, ks).astype(jnp.float32) * scale
        logits = jnp.where(valid[:, :, None, :], logits, -jnp.inf)
        p = jax.nn.softmax(logits, axis=-1).astype(v.dtype)
        return jnp.einsum('bthk,btkhd->bthd', p, vs)

    def blocks(a):
        return a.reshape((B, nblk, DSA_BLOCK) + a.shape[2:]).swapaxes(0, 1)

    starts = jnp.arange(nblk, dtype=jnp.int32) * DSA_BLOCK
    out = lax.map(block, (blocks(q), blocks(qi), blocks(wi), starts))
    return out.swapaxes(0, 1).reshape(B, S, H * Dh)

def short_conv(u, w):
    C = u.shape[-1]
    return lax.conv_general_dilated(
        u, w[:, None, :], window_strides=(1,), padding=[(CONV_WIDTH - 1, 0)],
        dimension_numbers=('NWC', 'WIO', 'NWC'), feature_group_count=C)

def fox_attention(q, k, v, log_f):
    B, S, H, Dh = q.shape
    nblk = S // FOX_BLOCK
    Fc = jnp.cumsum(log_f, axis=1).transpose(0, 2, 1)
    s_idx = jnp.arange(S, dtype=jnp.int32)
    scale = Dh ** -0.5

    def block(args):
        qb, Fb, t0 = args
        t = t0 + jnp.arange(FOX_BLOCK, dtype=jnp.int32)
        logits = jnp.einsum('bthd,bshd->bhts', qb, k).astype(jnp.float32) * scale
        logits = logits + Fb[..., None] - Fc[:, :, None, :]
        logits = jnp.where((s_idx[None, :] <= t[:, None])[None, None], logits, -jnp.inf)
        p = jax.nn.softmax(logits, axis=-1).astype(v.dtype)
        return jnp.einsum('bhts,bshd->bthd', p, v)

    qb = q.reshape(B, nblk, FOX_BLOCK, H, Dh).swapaxes(0, 1)
    Fb = Fc.reshape(B, H, nblk, FOX_BLOCK).transpose(2, 0, 1, 3)
    starts = jnp.arange(nblk, dtype=jnp.int32) * FOX_BLOCK
    out = lax.map(block, (qb, Fb, starts))
    return out.swapaxes(0, 1).reshape(B, S, H * Dh)

def even_mixer(x, positions, w_in, pool_w, pool_scale, w_out):
    B, S, _ = x.shape
    h = x @ w_in
    u_pool, q, k, v, qi, ki, wi = split_cols(h, EV_SIZES)
    a = pool_mixer(u_pool, pool_w, pool_scale)
    q = partial_rotary(q.reshape(B, S, DSA_HEADS, HEAD_DIM), positions)
    k = partial_rotary(k.reshape(B, S, DSA_HEADS, HEAD_DIM), positions)
    v = v.reshape(B, S, DSA_HEADS, HEAD_DIM)
    qi = partial_rotary(qi.reshape(B, S, IDX_HEADS, IDX_DIM), positions)
    ki = partial_rotary(ki[:, :, None, :], positions)[:, :, 0]
    wi = wi * (IDX_HEADS ** -0.5)
    b = dsa_attention(q, k, v, qi, ki, wi)
    return jnp.concatenate([a, b], axis=-1) @ w_out

def odd_mixer(x, w_in, conv_w, forget_b, w_out):
    B, S, _ = x.shape
    h = x @ w_in
    u, gate_b, gate_c, q, k, v, f_logit = split_cols(h, OD_SIZES)
    c = gate_b * short_conv(gate_c * u, conv_w)
    log_f = jax.nn.log_sigmoid((f_logit + forget_b).astype(jnp.float32))
    d = fox_attention(q.reshape(B, S, FOX_HEADS, HEAD_DIM), k.reshape(B, S, FOX_HEADS, HEAD_DIM),
                      v.reshape(B, S, FOX_HEADS, HEAD_DIM), log_f)
    return jnp.concatenate([c, d], axis=-1) @ w_out

def memory_cross_attention(x, mem, w_q, w_kv, w_o):
    B, S, _ = x.shape
    M = mem.shape[1]
    q = (x @ w_q).reshape(B, S, XA_HEADS, HEAD_DIM)
    kv = (mem @ w_kv).reshape(B, M, 2, XA_HEADS, HEAD_DIM)
    k, v = kv[:, :, 0], kv[:, :, 1]
    logits = jnp.einsum('bshd,bmhd->bhsm', q, k).astype(jnp.float32) * (HEAD_DIM ** -0.5)
    p = jax.nn.softmax(logits, axis=-1).astype(x.dtype)
    o = jnp.einsum('bhsm,bmhd->bshd', p, v).reshape(B, S, XA_WIDTH)
    return o @ w_o

def swiglu_ffn(x, w_in, w_out):
    gate, up = jnp.split(x @ w_in, 2, axis=-1)
    return (jax.nn.silu(gate) * up) @ w_out

def setup_inputs(seed: int = 0) -> dict:
    key = jax.random.key(seed)
    ks = jax.random.split(key, 20)

    def nrm(k, shape, scale):
        return jax.random.normal(k, shape, jnp.float32) * scale

    x = nrm(ks[0], (BATCH, SEQ, D_MODEL), 1.0)
    mem = nrm(ks[1], (BATCH, MEM_LEN, D_MODEL), 1.0)
    offs = jax.random.randint(ks[2], (BATCH,), 0, 64, dtype=jnp.int32) * CHUNK
    positions = (offs[:, None] + jnp.arange(SEQ, dtype=jnp.int32)[None, :]).astype(jnp.int32)
    return {
        "x": x,
        "mem": mem,
        "positions": positions,
        "ev_w_in": nrm(ks[3], (N_EVEN, D_MODEL, EV_IN), D_MODEL ** -0.5),
        "ev_pool_w": nrm(ks[4], (N_EVEN, POOL_GROUPS, POOL_GROUP_DIM, POOL_GROUP_DIM), POOL_GROUP_DIM ** -0.5),
        "ev_pool_scale": 1.0 + nrm(ks[5], (N_EVEN, HALF_WIDTH), 0.02),
        "ev_w_out": nrm(ks[6], (N_EVEN, MIX_WIDTH, D_MODEL), BETA * MIX_WIDTH ** -0.5),
        "od_w_in": nrm(ks[7], (N_ODD, D_MODEL, OD_IN), D_MODEL ** -0.5),
        "od_conv_w": nrm(ks[8], (N_ODD, CONV_WIDTH, CONV_DIM), CONV_WIDTH ** -0.5),
        "od_forget_b": FORGET_BIAS_INIT + nrm(ks[9], (N_ODD, FOX_HEADS), 0.1),
        "od_w_out": nrm(ks[10], (N_ODD, MIX_WIDTH, D_MODEL), BETA * MIX_WIDTH ** -0.5),
        "ca_w_q": nrm(ks[11], (DEPTH, D_MODEL, XA_WIDTH), D_MODEL ** -0.5),
        "ca_w_kv": nrm(ks[12], (DEPTH, D_MODEL, 2 * XA_WIDTH), D_MODEL ** -0.5),
        "ca_w_o": nrm(ks[13], (DEPTH, XA_WIDTH, D_MODEL), BETA * XA_WIDTH ** -0.5),
        "ffn_w_in": nrm(ks[14], (DEPTH, D_MODEL, 2 * FFN_HIDDEN), D_MODEL ** -0.5),
        "ffn_w_out": nrm(ks[15], (DEPTH, FFN_HIDDEN, D_MODEL), BETA * FFN_HIDDEN ** -0.5),
        "ln_g": 1.0 + nrm(ks[16], (DEPTH, 3, D_MODEL), 0.02),
        "ln_b": nrm(ks[17], (DEPTH, 3, D_MODEL), 0.02),
    }

def reference(x, mem, positions, ev_w_in, ev_pool_w, ev_pool_scale, ev_w_out,
              od_w_in, od_conv_w, od_forget_b, od_w_out,
              ca_w_q, ca_w_kv, ca_w_o, ffn_w_in, ffn_w_out, ln_g, ln_b):
    for i in range(DEPTH):
        j = i // 2
        if i % 2 == 0:
            m = even_mixer(x, positions, ev_w_in[j], ev_pool_w[j], ev_pool_scale[j], ev_w_out[j])
        else:
            m = odd_mixer(x, od_w_in[j], od_conv_w[j], od_forget_b[j], od_w_out[j])
        x = layer_norm(ALPHA * x + m, ln_g[i, 0], ln_b[i, 0])
        x = layer_norm(ALPHA * x + memory_cross_attention(x, mem, ca_w_q[i], ca_w_kv[i], ca_w_o[i]),
                       ln_g[i, 1], ln_b[i, 1])
        x = layer_norm(ALPHA * x + swiglu_ffn(x, ffn_w_in[i], ffn_w_out[i]), ln_g[i, 2], ln_b[i, 2])
    return x


_drawn_inputs = setup_inputs


def setup_inputs(seed=0):
    import zlib

    import numpy as np

    out = dict(_drawn_inputs(seed))
    spreads = {}
    factors = {'ev_pool_scale': 22.694, 'od_forget_b': 64.0}
    for name, (base, spread) in spreads.items():
        noise = np.random.default_rng([zlib.crc32(name.encode()), seed]).standard_normal(out[name].shape)
        drawn = base * np.exp(spread * noise) if base else spread * noise
        out[name] = __import__('jax').numpy.asarray(drawn.astype(out[name].dtype))
    for name, factor in factors.items():
        out[name] = (out[name] * factor).astype(out[name].dtype)
    return out
```

```python
from contextlib import ExitStack

import concourse.bass as bass
from concourse import mybir
import numpy as np

F32 = mybir.dt.float32
F32R = mybir.dt.float32r
I32 = mybir.dt.int32
ALU = mybir.AluOpType
ACT = mybir.ActivationFunctionType
AX = mybir.AxisListType.X

P = 128
D = 2048
S = 256
TB = S // P
KT = D // P
HALF = D // 2
HD = 128
HEADS = HALF // HD
XHEADS = 4
XW = XHEADS * HD
IDX_HEADS, IDX_DIM = 16, 64
TOPK = 64
CHUNK = 64
GROUPS = 4
GDIM = HALF // GROUPS
WINDOWS = (2, 4, 8, 16)
PAD = 16
PW = PAD + S
DEPTH = 2
FFN = 5632
FU = 512
UNITS = FFN // FU
PART_UNITS = 3
PARTS = UNITS // PART_UNITS
LAST_UNITS = UNITS - PARTS * PART_UNITS
ALPHA = float((2 * DEPTH) ** 0.25)
EPS = 1e-5
SCALE = float(HD) ** -0.5
ROPE_THETA = 500000.0
PANEL = 1024
RAW = 4
SPLIT = 4
GROUP = 4
NOT_ADMITTED = -2.0e38
TAKEN = -3.0e38
MASKED = -1.0e30
TWO_PI = 2.0 * np.pi

C_ID = 0
C_FREQ_Q, C_SIGN_Q, C_FREQ_I, C_SIGN_I = 128, 129, 130, 131
C_TRI = 132
C_ADMIT = C_TRI + P
C_INVC = C_ADMIT + P + S
C_END = C_INVC + GROUPS * PAD
V_G = 0
V_B = V_G + DEPTH * 3 * KT
V_SCALE = V_B + DEPTH * 3 * KT
V_CONV = V_SCALE + HALF // P
V_FB = V_CONV + 3 * HALF // P
V_END = V_FB + 1


def two_pi_parts():
    a = np.floor(TWO_PI * 2.0 ** 9) / 2.0 ** 9
    b = np.floor((TWO_PI - a) * 2.0 ** 21) / 2.0 ** 21
    return float(a), float(b), float(np.float32(TWO_PI - a - b))


class Tenant:

    def __init__(self, bank, need, drain, full):
        self.bank, self.need, self.drain, self.full = bank, need, drain, full


class Plan:

    def __init__(self):
        self.count = {"act": 0, "dve": 0, "staged": 0, "lo": 0}
        self.last = [None] * 8
        self.matmuls = 0

    def use(self, bank, drainer, times=1, panel=False):
        if not panel:
            self.matmuls += 1
        tenant = Tenant(bank, self.last[bank], None, None if panel else self.matmuls)
        if drainer:
            self.drained(tenant, drainer, times)
        return tenant

    def drained(self, tenant, drainer, times=1):
        self.count[drainer] += times
        tenant.drain = self.last[tenant.bank] = (drainer, self.count[drainer])

    def unit(self, half, drainers=("act",) * 4):
        return [self.use(4 * half + b, d, panel=True) for b, d in enumerate(drainers)]


def make_plan():
    p, use, first, tile, staged = Plan(), {}, {}, {}, {}
    at = 0

    def panels(name, count):
        nonlocal at
        first[name] = at
        at += count

    def split_now(name):
        tile[name], staged[name] = p.count["lo"], p.count["staged"]

    def lo(banks):
        return [p.use(b, "lo") for b in banks]

    def norm_tiles(name, half):
        split_now(name)
        use[name] = [p.use(4 * half + g % 4, "staged", times=2) for g in range(KT // 2)]
        p.count["lo"] += KT

    split_now("mem_t")
    use["mem_t"] = lo(g % 4 for g in range(KT // 2))
    use["kv", 0] = p.unit(1)
    panels(("kv", 0), KT)
    use["kv", 1] = p.unit(0)
    panels(("kv", 1), KT)
    split_now("x_t")
    use["x_t"] = lo(4 + g % 4 for g in range(KT // 2))
    half = 0
    for L in range(DEPTH):
        if L == 0:
            use["qi", L] = p.unit(half)
            panels(("qi", L), KT)
            use["kw"] = [p.use(4 * (1 - half) + 3, "act", panel=True)]
            panels("kw", 2)
            use["q", L] = p.unit(1 - half)
            panels(("q", L), KT)
            use["wi_t"] = p.use(4 * half, "dve")
            use["idx"] = []
            for i in range(IDX_HEADS):
                even = p.use(4 * half + 2 * (i % 2), None, panel=True)
                odd = p.use(4 * half + 2 * (i % 2) + 1, "act")
                p.last[even.bank] = even.drain = odd.drain
                use["idx"].append((even, odd))
            use["k", L] = p.unit(1 - half)
            panels(("k", L), KT)
            use["v", L] = p.unit(half)
            panels(("v", L), KT)
            fill, att = half, 1 - half
        else:
            use["q", L] = p.unit(half)
            panels(("q", L), KT)
            use["k", L] = p.unit(1 - half)
            panels(("k", L), KT)
            use["v", L] = p.unit(half)
            panels(("v", L), KT)
            use["f"] = [p.use(4 * (1 - half), "dve", panel=True)]
            panels("f", 1)
            use["ft"] = p.use(4 * (1 - half) + 1, "dve")
            fill, att = 1 - half, half
        use["z", L], use["pt", L], use["o", L] = [], [], []
        panels(("u", L), KT)
        if L == 1:
            panels(("gc", L), KT)
            panels(("gb", L), KT)
        split_now(("o", L))
        for h in range(HEADS + 1):
            if h == 0:
                use["u", L] = p.unit(fill, (None,) * 4)
            if L == 1 and h == HEADS // 2:
                use["gc", L] = p.unit(fill, (None,) * 4)
            if h < HEADS:
                use["z", L].append(p.use(4 * att + h % 2, "dve"))
            if h > 0:
                use["pt", L].append(p.use(4 * att + 2, "act"))
            if h == (HEADS if L == 0 else HEADS // 2 - 1):
                for t in use["u", L]:
                    p.drained(t, "act")
            if h > 0:
                use["o", L].append(p.use(4 * att + 3, "lo"))
            if L == 1 and h == HEADS - 1:
                for t in use["gc", L]:
                    p.drained(t, "dve")
        split_now(("branch", L))
        if L == 0:
            use["out", L, 0] = p.unit(fill, ("dve",) * 4)
            use["pool"] = [p.use(4 * att + g, "staged") for g in range(GROUPS)]
        else:
            use["gb", L] = p.unit(fill, ("staged",) * 4)
            use["out", L, 0] = p.unit(fill, ("dve",) * 4)
        p.count["lo"] += 4
        panels(("out", L, 0), KT)
        use["out", L, 1] = p.unit(att, ("dve",) * 4)
        panels(("out", L, 1), KT)
        a, b = fill, att
        norm_tiles(("ln_t", L, 0), a)
        use["xq", L] = [p.use(4 * b + i, "act", panel=True) for i in range(2)]
        panels(("xq", L), KT // 2)
        use["xz", L] = [p.use(4 * a + h, "act") for h in range(XHEADS)]
        use["xpt", L], use["xo", L] = [], []
        split_now(("xo", L))
        for h in range(XHEADS):
            use["xpt", L].append(p.use(4 * b + h % 2, "act"))
            use["xo", L].append(p.use(4 * b + 2 + h % 2, "lo"))
        use["xout", L, 0] = p.unit(a, ("dve",) * 4)
        panels(("xout", L, 0), XHEADS)
        use["xout", L, 1] = p.unit(b, ("dve",) * 4)
        panels(("xout", L, 1), XHEADS)
        norm_tiles(("ln_t", L, 1), a)
        for i in range(PARTS + 1):
            before = dict(p.count), at
            s = b
            for j in range(PART_UNITS if i < PARTS else LAST_UNITS):
                split_now(("in", L, i, j))
                use["in", L, i, j] = p.unit(s, ("act", "act", "staged", "staged"))
                p.count["lo"] += 2
                panels(("in", L, i, j), KT)
                s = 1 - s
            for c in range(2):
                use["down", L, i, c] = p.unit(s, ("dve",) * 4)
                panels(("down", L, i, c), (PART_UNITS if i < PARTS else LAST_UNITS) * GROUP)
                s = 1 - s
            if i < PARTS:
                use["stride"] = {w: p.count[w] - before[0][w] for w in p.count}
                first["stride"] = at - before[1]
        last = 1 - s
        first["next", L] = at
        if L < DEPTH - 1:
            norm_tiles(("ln_t", L, 2), 1 - last)
        half = last
    for L in range(DEPTH):
        for j in range(PART_UNITS):
            for b, t in enumerate(use["in", L, 0, j]):
                who, value = use["in", L, 1, j][b].need
                t.need = (who, value - use["stride"][who])
        for c in range(2):
            for b, t in enumerate(use["down", L, 0, c]):
                who, value = use["down", L, 1, c][b].need
                t.need = (who, value - use["stride"][who])
    return p, use, first, tile, staged


def build(nc, a):
    plan, use, first, tile, staged = make_plan()
    stride = use["stride"]
    consts, vectors, pos = a["shape_constants"], a["vectors"], a["positions"]
    x_in, mem_in, out = a["x"], a["mem"], a["out"]
    x_view = x_in.rearrange("o (b p) d -> p (o b) d", p=P)
    mem_view = mem_in.rearrange("o (b p) d -> p (o b) d", p=P)
    out_view = out.rearrange("o (b p) d -> p (o b) d", p=P)
    w_mix = [a["ev_w_in"][0], a["od_w_in"][0]]
    w_out = [a["ev_w_out"][0], a["od_w_out"][0]]
    w_down = a["ffn_w_out"]
    w_up = a["ffn_w_in"].rearrange("l k (g n) -> l k g n", g=2)
    pool_w = a["ev_pool_w"].rearrange("o g (t p) d -> p (o g t) d", p=P)

    with ExitStack() as ctx:
        def sb(name, shape, dt=F32):
            return ctx.enter_context(nc.sbuf_tensor(name, shape, dt))

        def sem(name):
            return ctx.enter_context(nc.semaphore(name))

        raw = sb("raw", [P, RAW, PANEL])
        w_hi = sb("w_hi", [P, SPLIT, PANEL], F32R)
        w_lo = sb("w_lo", [P, SPLIT, PANEL], F32R)
        x = sb("x_tok", [P, TB, D])
        x_hi = sb("x_hi", [P, KT * S], F32R)
        x_lo = sb("x_lo", [P, KT * S], F32R)
        c_hi = sb("c_hi", [P, KT * S], F32R)
        c_lo = sb("c_lo", [P, KT * S], F32R)
        k_mem = sb("k_mem", [P, DEPTH, XHEADS, S])
        v_mem = sb("v_mem", [P, DEPTH, TB, XW])
        area_a = sb("area_a", [P, HALF // P, PW])
        area_b = sb("area_b", [P, HALF // P, S])
        area_cd = sb("area_cd", [P, 2, HALF // P * S])
        stage = sb("stage", [P, 2, 2 * S])
        scratch = sb("scratch", [P, XHEADS * TB * S])
        bias = sb("bias", [P, 2, P + S])
        cst = sb("cst", [P, C_END])
        vec = sb("vec", [P, V_END])
        small = sb("small", [P, 256])
        tall = sb("tall", [P, 4, S])
        ki = sb("ki", [P, S])

        psum = ctx.enter_context(nc.psum_tensor("psum", [P, 8, 512], F32))

        q_sb = area_b
        k_sb = area_cd[:, 0, :].rearrange("p (h s) -> p h s", h=HEADS)
        v_sb = area_cd[:, 1, :].rearrange("p (b n) -> p b n", b=TB)
        qi_sb = area_cd[:, 1, :].rearrange("p (h s) -> p h s", h=HEADS)
        mem_tok = area_cd
        gain, offset = area_cd[:, 0, :], area_cd[:, 1, :]
        ident = cst[:, C_ID:C_ID + P]
        relu = scratch[:, 0:1024].rearrange("p (b n) -> p b n", b=2)
        rope_tmp = scratch[:, 0:512]
        tables = scratch[:, 1024:2048].rearrange("p (t s) -> p t s", t=4)
        probs = scratch[:, 0:1024].rearrange("p (b n) -> p b n", b=2)
        probs_t = scratch[:, 1024:2048].rearrange("p (b n) -> p b n", b=2)
        ping = scratch[:, 0:2 * PW].rearrange("p (t n) -> p t n", t=2)
        pong = scratch[:, 2 * PW:4 * PW].rearrange("p (t n) -> p t n", t=2)
        gate = scratch[:, 0:1024].rearrange("p (b n) -> p b n", b=2)

        def xprobs(h):
            return scratch[:, 512 * h:512 * (h + 1)].rearrange("p (b n) -> p b n", b=TB)

        def xprobs_t(h):
            return area_b[:, 4 + 2 * (h % 2):6 + 2 * (h % 2), :].rearrange("p t n -> p (t n)")

        score, work = bias[:, 0, :], bias[:, 1, :]
        decay, neg_decay = tall[0:HEADS, 0, :], tall[0:HEADS, 1, :]
        dtmp, ones8 = tall[0:HEADS, 2, :], tall[0:HEADS, 3, :]
        wi_tok = small[:, 0:32].rearrange("p (b h) -> p b h", b=TB)
        decay_tok = small[:, 32:48].rearrange("p (b h) -> p b h", b=TB)
        neg_max = small[:, 48:80].rearrange("p (h b) -> p h b", b=TB)
        sums = small[:, 80:112].rearrange("p (h b) -> p h b", b=TB)
        rec = small[:, 112:144].rearrange("p (h b) -> p h b", b=TB)
        top8 = small[:, 144:160].rearrange("p (b n) -> p b n", b=TB)
        stats = small[:, 160:208].rearrange("p (b c n) -> p b c n", b=TB, c=4)
        mv = small[:, 208:212].rearrange("p (b n) -> p b n", b=TB)
        var, dev, rstd = small[:, 212:214], small[:, 214:216], small[:, 216:218]
        warm = small[:, 218:220]

        consts_in, vectors_in, positions_in = sem("consts_in"), sem("vectors_in"), sem("positions_in")
        x_arrived, mem_arrived = sem("x_arrived"), sem("mem_arrived")
        gain_in, pool_w_in, stored = sem("gain_in"), sem("pool_w_in"), sem("stored")
        landed = [sem(f"landed{i}") for i in range(RAW)]
        hi_done, lo_done = sem("hi_done"), sem("lo_done")
        panels_used = sem("panels_used")
        matmuls_done = sem("matmuls_done")
        act_drained, dve_drained = sem("act_drained"), sem("dve_drained")
        tile_staged, tile_hi, tile_lo = sem("tile_staged"), sem("tile_hi"), sem("tile_lo")
        tables_angle, tables_ready = sem("tables_angle"), sem("tables_ready")
        rope_done, index_summed, mask_ready = sem("rope_done"), sem("index_summed"), sem("mask_ready")
        maxima_ready, exp_done, probs_ready = sem("maxima_ready"), sem("exp_done"), sem("probs_ready")
        pooled, pool_read = sem("pooled"), sem("pool_read")
        gate_free, gated = sem("gate_free"), sem("gated")
        decay_in, decay_exp, decay_log, decay_ready = (
            sem("decay_in"), sem("decay_exp"), sem("decay_log"), sem("decay_ready"))
        variance_ready, deviation_ready, normalized = (
            sem("variance_ready"), sem("deviation_ready"), sem("normalized"))
        affine_done, zeroed = sem("affine_done"), sem("zeroed")
        dve_step, act_step, pool_step = sem("dve_step"), sem("act_step"), sem("pool_step")

        drained = {"act": act_drained, "dve": dve_drained, "staged": tile_staged, "lo": tile_lo}

        def wait_drained(eng, tenant, part=None):
            if tenant.need is not None:
                who, value = tenant.need
                eng.wait_ge(drained[who], value if part is None else part * stride[who] + value)

        def slot(c):
            return c % RAW

        def later(value, laps, per_lap):
            return value if isinstance(laps, int) and laps == 0 else laps * per_lap + value

        def attention_order(L):
            return list(range(HEADS, KT)) + list(range(HEADS))

        block = ctx.enter_context(nc.Block())

        @block.sync
        def _(sp):
            def panel(c, laps, src, shape=None):
                if c >= RAW:
                    sp.wait_ge(lo_done, later(c - RAW + 1, laps, GROUP))
                dst = raw[:, slot(c), :]
                if shape:
                    dst = dst[:, 0:shape[0] * shape[1]].rearrange("p (k n) -> p k n", n=shape[1])
                sp.dma_start(dst, src).then_inc(landed[slot(c)], 16)

            def columns(c0, w, col, width=PANEL, kt=KT):
                peeled = 1 if c0 < RAW else 0
                for j in range(peeled * GROUP):
                    panel(c0 + j, 0, w[j * P:(j + 1) * P, col:col + width])
                with sp.Fori(peeled, kt // GROUP) as g:
                    for j in range(GROUP):
                        if peeled:
                            sp.wait_ge(lo_done, g * GROUP + (j - RAW + 1))
                            sp.dma_start(raw[:, slot(j), :], w[bass.ds(g * (GROUP * P) + j * P, P), col:col + width]
                                         ).then_inc(landed[slot(j)], 16)
                        else:
                            panel(c0 + j, g, w[bass.ds(g * (GROUP * P) + j * P, P), col:col + width])

            def rows_in_order(c0, w, col, order):
                for j, t in enumerate(order):
                    panel(c0 + j, 0, w[t * P:(t + 1) * P, col:col + PANEL])

            def gain_and_offset(i, before, value):
                sp.wait_ge(before, value)
                sp.dma_start(gain, a["ln_g"][i // 3, i % 3:i % 3 + 1, :].to_broadcast([P, D])).then_inc(gain_in, 16)
                sp.dma_start(offset, a["ln_b"][i // 3, i % 3:i % 3 + 1, :].to_broadcast([P, D])).then_inc(gain_in, 16)

            sp.dma_start(cst[:, :], consts).then_inc(consts_in, 16)
            for b in range(TB):
                sp.dma_start(mem_tok[:, b, :], mem_view[:, b, :]).then_inc(mem_arrived, 16)
            sp.dma_start(vec[:, :], vectors).then_inc(vectors_in, 16)
            sp.dma_start(tall[:, 0, :].bitcast(I32), pos.to_broadcast([P, S])).then_inc(positions_in, 16)
            columns(first["kv", 0], a["ca_w_kv"][0], 0)
            for b in range(TB):
                sp.dma_start(x[:, b, :], x_view[:, b, :]).then_inc(x_arrived, 16)
            columns(first["kv", 1], a["ca_w_kv"][1], 0)
            for L in range(DEPTH):
                w = w_mix[L]
                if L == 0:
                    columns(first["qi", 0], w, 4 * HALF)
                    kw = w[:, 4 * HALF + HALF:4 * HALF + HALF + IDX_DIM + IDX_HEADS].rearrange(
                        "(k p) n -> p k n", p=P)
                    for j in range(2):
                        panel(first["kw"] + j, 0, kw[:, 8 * j:8 * j + 8, :], (8, IDX_DIM + IDX_HEADS))
                    columns(first["q", L], w, HALF)
                    columns(first["k", L], w, 2 * HALF)
                    columns(first["v", L], w, 3 * HALF)
                    columns(first["u", L], w, 0)
                else:
                    columns(first["q", L], w, 3 * HALF)
                    columns(first["k", L], w, 4 * HALF)
                    columns(first["v", L], w, 5 * HALF)
                    panel(first["f"], 0, w[:, 6 * HALF:6 * HALF + HEADS].rearrange("(k p) n -> p k n", p=P),
                          (KT, HEADS))
                    columns(first["u", L], w, 0)
                    columns(first["gc", L], w, 2 * HALF)
                    columns(first["gb", L], w, HALF)
                order = attention_order(L)
                rows_in_order(first["out", L, 0], w_out[L], 0, order[0:GROUP])
                if L == 0:
                    sp.wait_ge(matmuls_done, use["z", L][-1].full)
                    sp.dma_start(area_b[:, :, :], pool_w).then_inc(pool_w_in, 16)
                rows_in_order(first["out", L, 0] + GROUP, w_out[L], 0, order[GROUP:])
                gain_and_offset(3 * L, matmuls_done, use["o", L][-1].full)
                rows_in_order(first["out", L, 1], w_out[L], HALF, attention_order(L))
                wq = a["ca_w_q"][L].rearrange("(k p) n -> p k n", p=P)
                for j in range(KT // 2):
                    panel(first["xq", L] + j, 0, wq[:, 2 * j:2 * j + 2, :], (2, XW))
                for c in range(2):
                    rows_in_order(first["xout", L, c], a["ca_w_o"][L], c * HALF, range(XHEADS))
                gain_and_offset(3 * L + 1, affine_done, 3 * L + 2)

                def part(i, units, base, reg):
                    laps = 0 if reg is None else reg * (first["stride"] // GROUP)
                    for j in range(units):
                        c0 = first["in", L, i, j]
                        with sp.Fori(0, KT // GROUP) as g:
                            for t in range(GROUP):
                                rows = bass.ds(g * (GROUP * P) + t * P, P)
                                if reg is None:
                                    cols = slice((base + j) * FU, (base + j + 1) * FU)
                                else:
                                    cols = bass.ds(reg * (PART_UNITS * FU) + j * FU, FU)
                                src = w_up[L, rows, :, cols]
                                panel(c0 + t, g if reg is None else g + laps, src, (2, FU))
                    for c in range(2):
                        c0 = first["down", L, i, c]
                        with sp.Fori(0, units) as g:
                            for t in range(GROUP):
                                if reg is None:
                                    row = g * (GROUP * P) + (base * FU + t * P)
                                else:
                                    row = g * (GROUP * P) + reg * (PART_UNITS * FU) + t * P
                                src = w_down[L, bass.ds(row, P), c * HALF:(c + 1) * HALF]
                                panel(c0 + t, g if reg is None else g + laps, src)

                with sp.Fori(0, PARTS) as i:
                    part(0, PART_UNITS, 0, i)
                part(PARTS, LAST_UNITS, PARTS * PART_UNITS, None)
                if L < DEPTH - 1:
                    gain_and_offset(3 * L + 2, affine_done, 3 * L + 3)
                else:
                    gain_and_offset(3 * L + 2, affine_done, 3 * L + 3)
            for b in range(TB):
                sp.wait_ge(affine_done, 3 * DEPTH + 1 + b)
                sp.dma_start(out_view[:, b, :], x[:, b, :]).then_inc(stored, 16)
            sp.wait_ge(stored, 16 * TB)

        @block.gpsimd
        def _(pool):
            steps = 0

            def step(ins):
                nonlocal steps
                steps += 1
                ins.then_inc(pool_step, 1)
                pool.wait_ge(pool_step, steps)

            def split_low(c, count):
                pool.wait_ge(lo_done, c)
                with pool.Fori(0, count // GROUP) as g:
                    for j in range(GROUP):
                        s = slot(c + j)
                        pool.wait_ge(hi_done, g * GROUP + (c + j + 1))
                        pool.tensor_tensor(w_lo[:, s, :], raw[:, s, :], w_hi[:, s, :].bitcast(F32),
                                           ALU.subtract).then_inc(lo_done, 1)

            pool.memset(area_a[:, :, 0:PAD], 0.0).then_inc(zeroed, 1)

            pool.wait_ge(positions_in, 16)
            pool.wait_ge(consts_in, 16)
            pos_f = tall[:, 1, :]
            step(pool.tensor_copy(pos_f, tall[:, 0, :].bitcast(I32)))
            magic = 1.5 * 2.0 ** 23
            for t, freq in ((0, C_FREQ_Q), (1, C_FREQ_I)):
                ang, n, m, tmp = tables[:, 2 * t + 1, :], tall[:, 2, :], tall[:, 3, :], tall[:, 0, :]
                step(pool.tensor_scalar(ang, pos_f, cst[:, freq:freq + 1], None, ALU.mult))
                step(pool.tensor_scalar(n, ang, 1.0 / TWO_PI, magic, ALU.mult, ALU.add))
                step(pool.tensor_scalar(n, n, -magic, None, ALU.add))
                step(pool.tensor_scalar(m, n, 1.0 / 4096, magic, ALU.mult, ALU.add))
                step(pool.tensor_scalar(m, m, -magic, 4096.0, ALU.add, ALU.mult))
                step(pool.tensor_tensor(n, n, m, ALU.subtract))
                for part in two_pi_parts():
                    for f in (m, n):
                        step(pool.tensor_scalar(tmp, f, -part, None, ALU.mult))
                        step(pool.tensor_tensor(ang, ang, tmp, ALU.add))
                limit = 3.1415925
                step(pool.tensor_scalar(ang, ang, limit, -limit, ALU.min, ALU.max))
                step(pool.tensor_scalar(tmp, ang, 0.0, 2.0, ALU.max, ALU.mult))
                step(pool.tensor_tensor(tmp, tmp, ang, ALU.subtract))
                pool.tensor_scalar(tables[:, 2 * t, :], tmp, -1.0, TWO_PI / 4,
                                   ALU.mult, ALU.add).then_inc(tables_angle, 1)
                pool.wait_ge(tables_angle, t + 1)

            def scale_x():
                pool.tensor_scalar(x[:, :, :], x[:, :, :], ALPHA, None, ALU.mult).then_inc(affine_done, 1)

            def affine(i, last_transpose):
                pool.wait_ge(gain_in, 32 * (i + 1))
                pool.wait_ge(matmuls_done, last_transpose)
                for b in range(TB):
                    step(pool.tensor_tensor(x[:, b, :], x[:, b, :], gain, ALU.mult))
                    step(pool.tensor_tensor(x[:, b, :], x[:, b, :], offset, ALU.add))
                scale_x()

            pool.wait_ge(x_arrived, 16 * TB)
            pool.wait_ge(matmuls_done, use["x_t"][-1].full)
            scale_x()
            for L in range(DEPTH):
                if L == 0:
                    split_low(first["q", L], 4 * KT)
                else:
                    split_low(first["u", L], 3 * KT)
                affine(3 * L, use["ln_t", L, 0][-1].full)
                affine(3 * L + 1, use["ln_t", L, 1][-1].full)
                if L < DEPTH - 1:
                    affine(3 * L + 2, use["ln_t", L, 2][-1].full)

        @block.scalar
        def _(act):
            def split_high(c, count):
                def one(c, laps):
                    s = slot(c)
                    act.wait_ge(landed[s], later(16 * (c // RAW + 1), laps, 16))
                    if c >= SPLIT:
                        act.wait_ge(panels_used, later(c - SPLIT + 1, laps, GROUP))
                    act.activation(w_hi[:, s, :], raw[:, s, :], ACT.Copy).then_inc(hi_done, 1)
                if count % GROUP == 0 and count > GROUP and c >= SPLIT:
                    with act.Fori(0, count // GROUP) as g:
                        for j in range(GROUP):
                            one(c + j, g)
                else:
                    for j in range(count):
                        one(c + j, 0)

            def high_from_bank(t, ps, dst):
                act.activation(dst, ps, ACT.Copy).then_inc(tile_hi, 1)

            def high_from_stage(t, r, dst, width):
                act.wait_ge(tile_staged, r + 1)
                act.activation(dst, stage[:, t % 2, 0:width], ACT.Copy).then_inc(tile_hi, 1)

            def tiles2(dst, j):
                return dst[:, 2 * j * S:2 * (j + 1) * S]

            def drain(tenant, dst, src, panel_end=None, func=ACT.Copy, scale=1.0):
                act.activation(dst, src, func, scale=scale).then_inc(act_drained, 1)

            act.wait_ge(zeroed, 1)
            split_high(first["kv", 0], GROUP)
            for g, t in enumerate(use["mem_t"]):
                act.wait_ge(matmuls_done, t.full)
                high_from_bank(tile["mem_t"] + g, psum[:, t.bank, :], tiles2(c_hi, g))
            split_high(first["kv", 0] + GROUP, KT - GROUP)

            def evacuate_kv(L):
                act.wait_ge(panels_used, first["kv", L] + KT)
                for b, t in enumerate(use["kv", L]):
                    dst = (k_mem[:, L, 2 * b:2 * b + 2, :].rearrange("p h s -> p (h s)") if b < 2
                           else v_mem[:, L, b - 2, :])
                    drain(t, dst, psum[:, t.bank, :])

            split_high(first["kv", 1], GROUP)
            evacuate_kv(0)
            split_high(first["kv", 1] + GROUP, KT - GROUP)
            split_high(first["qi", 0], GROUP)
            evacuate_kv(1)
            for g, t in enumerate(use["x_t"]):
                act.wait_ge(matmuls_done, t.full)
                high_from_bank(tile["x_t"] + g, psum[:, t.bank, :], tiles2(x_hi, g))
            act.wait_ge(tables_angle, 2)
            act.activation(tables[:, :, :], tables[:, :, :], ACT.Sin).then_inc(tables_ready, 1)

            def evacuate(name, L, dst):
                act.wait_ge(panels_used, first[name, L] + KT)
                for b, t in enumerate(use[name, L]):
                    drain(t, dst(b), psum[:, t.bank, :])

            def pair(area):
                return lambda b: area[:, 2 * b:2 * b + 2, :].rearrange("p h s -> p (h s)")

            def u_pair(b):
                return area_a[:, 2 * b:2 * b + 2, PAD:PW]

            def evacuate_u(L):
                act.wait_ge(panels_used, first["u", L] + KT)
                for b, t in enumerate(use["u", L]):
                    drain(t, u_pair(b), psum[:, t.bank, :].rearrange("p (h s) -> p h s", h=2))

            def evacuate_v(L):
                act.wait_ge(panels_used, first["v", L] + KT)
                for b, t in enumerate(use["v", L]):
                    drain(t, v_sb[:, b // 2, (b % 2) * 512:(b % 2 + 1) * 512], psum[:, t.bank, :])

            def head_probs(L, h):
                act.wait_ge(maxima_ready, maxima0 + h + 1)
                z = probs[:, h % 2, :]
                act.activation(z[:, 0:P], z[:, 0:P], ACT.Exp, bias=neg_max[:, h, 0:1], scale=SCALE,
                               accum_out=sums[:, h, 0:1]).then_inc(exp_done, 1)
                act.activation(z[:, P:P + S], z[:, P:P + S], ACT.Exp, bias=neg_max[:, h, 1:2], scale=SCALE,
                               accum_out=sums[:, h, 1:2]).then_inc(exp_done, 1)

            maxima0 = 0
            for L in range(DEPTH):
                maxima0 = L * (HEADS + XHEADS)
                if L == 0:
                    split_high(first["qi", 0] + GROUP, KT - GROUP)
                    split_high(first["kw"], 2)
                    split_high(first["q", L], 2)
                    evacuate("qi", L, pair(qi_sb))
                    split_high(first["q", L] + 2, 2)
                    act.wait_ge(panels_used, first["kw"] + 2)
                    ps = psum[:, use["kw"][0].bank, 0:S]
                    act.activation(ki[0:IDX_DIM, :], ps[0:IDX_DIM, :], ACT.Copy).then_inc(act_step, 1)
                    act.activation(ki[IDX_DIM:2 * IDX_DIM, :], ps[0:IDX_DIM, :], ACT.Copy).then_inc(act_step, 1)
                    drain(use["kw"][0], tall[IDX_DIM:IDX_DIM + IDX_HEADS, 0, :],
                          ps[IDX_DIM:IDX_DIM + IDX_HEADS, :])
                    split_high(first["q", L] + GROUP, KT - GROUP)
                    split_high(first["k", L], GROUP)
                    evacuate("q", L, pair(q_sb))
                    for i, (even, t) in enumerate(use["idx"]):
                        act.wait_ge(matmuls_done, t.full)
                        if i >= 2:
                            act.wait_ge(index_summed, i - 1)
                        width = P * (i % TB + 1)
                        drain(t, relu[:, i % 2, 0:2 * width].rearrange("p (h n) -> p h n", h=2),
                              psum[:, even.bank:even.bank + 2, 0:width], func=ACT.Relu,
                              scale=IDX_DIM ** -0.5)
                    split_high(first["k", L] + GROUP, KT - GROUP)
                    split_high(first["v", L], GROUP)
                    evacuate("k", L, pair(k_sb))
                    split_high(first["v", L] + GROUP, KT - GROUP)
                    split_high(first["u", L], GROUP)
                    evacuate_v(L)
                else:
                    split_high(first["q", L] + GROUP, KT - GROUP)
                    split_high(first["k", L], GROUP)
                    act.wait_ge(affine_done, 3 * L + 1)
                    evacuate("q", L, pair(q_sb))
                    split_high(first["k", L] + GROUP, KT - GROUP)
                    split_high(first["v", L], GROUP)
                    evacuate("k", L, pair(k_sb))
                    split_high(first["v", L] + GROUP, KT - GROUP)
                    split_high(first["f"], 1)
                    split_high(first["u", L], GROUP - 1)
                    evacuate_v(L)
                    act.wait_ge(decay_in, 1)
                    act.activation(dtmp, dtmp, ACT.Exp, scale=-1.0).then_inc(decay_exp, 1)
                    act.wait_ge(decay_exp, 1)
                    act.activation(dtmp, dtmp, ACT.Ln, bias=1.0).then_inc(decay_log, 1)
                    split_high(first["u", L] + GROUP - 1, 1)
                per_head = 2 if L == 0 else 4
                ahead = first["u", L] + GROUP
                for h in range(HEADS + 1):
                    if h > 0:
                        t = use["pt", L][h - 1]
                        act.wait_ge(matmuls_done, t.full)
                        drain(t, probs_t[:, (h - 1) % 2, 0:3 * P], psum[:, t.bank, 0:3 * P])
                    if h < HEADS:
                        head_probs(L, h)
                        split_high(ahead, per_head // 2)
                        ahead += per_head // 2
                    elif L == 0:
                        evacuate_u(L)
                    if L == 1 and h == HEADS // 2 - 1:
                        split_high(ahead, per_head // 2)
                        ahead += per_head // 2
                        evacuate_u(L)
                    if h > 0:
                        t = use["o", L][h - 1]
                        act.wait_ge(matmuls_done, t.full)
                        j = HEADS + h - 1
                        high_from_bank(tile["o", L] + h - 1, psum[:, t.bank, 0:S], c_hi[:, j * S:(j + 1) * S])
                    if h < HEADS and not (L == 1 and h == HEADS // 2 - 1):
                        split_high(ahead, per_head // 2)
                        ahead += per_head // 2
                if L == 1:
                    split_high(ahead, KT - GROUP)
                    split_high(first["out", L, 0], GROUP)
                if L == 0:
                    split_high(first["out", L, 0] + GROUP, GROUP)
                for g in range(4):
                    high_from_stage(tile["branch", L] + g, staged["branch", L] + g, tiles2(c_hi, g), 2 * S)
                if L == 1:
                    split_high(first["out", L, 0] + GROUP, GROUP)
                split_high(first["out", L, 0] + 2 * GROUP, 2 * GROUP)
                split_high(first["out", L, 1], KT)

                def warm_sqrt():
                    act.activation(warm[:, 1:2], cst[:, C_ID:C_ID + 1], ACT.Sqrt).then_inc(act_step, 1)

                def deviation(i):
                    act.wait_ge(variance_ready, i + 1)
                    act.activation(dev, var, ACT.Sqrt).then_inc(deviation_ready, 1)

                def norm_tiles(L, i):
                    for j in range(KT):
                        high_from_stage(tile["ln_t", L, i] + j, staged["ln_t", L, i] + j,
                                        x_hi[:, j * S:(j + 1) * S], S)

                split_high(first["xq", L], GROUP)
                warm_sqrt()
                deviation(3 * L)
                norm_tiles(L, 0)
                split_high(first["xq", L] + GROUP, GROUP)
                split_high(first["xout", L, 0], GROUP)
                act.wait_ge(panels_used, first["xq", L] + KT // 2)
                for b, t in enumerate(use["xq", L]):
                    drain(t, area_b[:, 2 * b:2 * b + 2, :].rearrange("p h s -> p (h s)"), psum[:, t.bank, :])
                for h, t in enumerate(use["xz", L]):
                    act.wait_ge(maxima_ready, maxima0 + HEADS + h + 1)
                    z = xprobs(h)
                    for b in range(TB):
                        ins = act.activation(z[:, b, :], psum[:, t.bank, b * S:(b + 1) * S], ACT.Exp,
                                             bias=neg_max[:, HEADS + h, b:b + 1], scale=SCALE,
                                             accum_out=sums[:, HEADS + h, b:b + 1])
                        ins.then_inc(exp_done if b == 0 else act_drained, 1)
                for h in range(XHEADS):
                    t = use["xpt", L][h]
                    act.wait_ge(matmuls_done, t.full)
                    drain(t, xprobs_t(h), psum[:, t.bank, :])
                    if h > 0:
                        t = use["xo", L][h - 1]
                        act.wait_ge(matmuls_done, t.full)
                        high_from_bank(tile["xo", L] + h - 1, psum[:, t.bank, 0:S], c_hi[:, (h - 1) * S:h * S])
                t = use["xo", L][-1]
                act.wait_ge(matmuls_done, t.full)
                high_from_bank(tile["xo", L] + 3, psum[:, t.bank, 0:S], c_hi[:, 3 * S:4 * S])
                split_high(first["xout", L, 1], GROUP)
                split_high(first["in", L, 0, 0], GROUP)
                warm_sqrt()
                deviation(3 * L + 1)
                norm_tiles(L, 1)

                def ffn_part(i, units, reg):
                    laps = 0 if reg is None else reg * (first["stride"] // GROUP)

                    def split(c, count):
                        if reg is None and count > GROUP:
                            with act.Fori(0, count // GROUP) as g:
                                split_group(c, g)
                        elif count > GROUP:
                            with act.Fori(0, count // GROUP) as g:
                                split_group(c, g + laps)
                        elif count:
                            split_group(c, laps)

                    def split_group(c, laps):
                        for j in range(GROUP):
                            s = slot(c + j)
                            act.wait_ge(landed[s], later(16 * ((c + j) // RAW + 1), laps, 16))
                            act.wait_ge(panels_used, later(c + j - SPLIT + 1, laps, GROUP))
                            act.activation(w_hi[:, s, :], raw[:, s, :], ACT.Copy).then_inc(hi_done, 1)

                    def count(value, per_part):
                        return value if reg is None else reg * per_part + value

                    for j in range(units):
                        c0 = first["in", L, i, j]
                        split(c0 + GROUP, KT - GROUP)
                        after = first["in", L, i, j + 1] if j + 1 < units else first["down", L, i, 0]
                        split(after, GROUP)
                        act.wait_ge(panels_used, count(c0 + KT, first["stride"]))
                        for b, t in enumerate(use["in", L, i, j][0:2]):
                            drain(t, gate[:, b, :], psum[:, t.bank, :], func=ACT.Silu)
                        for b in range(2):
                            k = tile["in", L, i, j] + b
                            act.wait_ge(tile_staged, count(staged["in", L, i, j] + b + 1, stride["staged"]))
                            act.activation(tiles2(c_hi, 2 * j + b), stage[:, k % 2, :],
                                           ACT.Copy).then_inc(tile_hi, 1)
                    for c in range(2):
                        c0 = first["down", L, i, c]
                        split(c0 + GROUP, (units - 1) * GROUP)
                        if c == 0:
                            split(first["down", L, i, 1], GROUP)
                        elif i < PARTS:
                            split(c0 + units * GROUP, GROUP)

                with act.Fori(0, PARTS) as i:
                    ffn_part(0, PART_UNITS, i)
                ffn_part(PARTS, LAST_UNITS, None)
                if L < DEPTH - 1:
                    split_high(first["q", L + 1], GROUP)
                warm_sqrt()
                deviation(3 * L + 2)
                if L < DEPTH - 1:
                    norm_tiles(L, 2)

        @block.vector
        def _(dve):
            steps = 0

            def step(ins):
                nonlocal steps
                steps += 1
                ins.then_inc(dve_step, 1)
                dve.wait_ge(dve_step, steps)

            def split_group(c, laps):
                for j in range(GROUP):
                    s = slot(c + j)
                    dve.wait_ge(hi_done, later(c + j + 1, laps, GROUP))
                    dve.tensor_tensor(w_lo[:, s, :], raw[:, s, :], w_hi[:, s, :].bitcast(F32),
                                      ALU.subtract).then_inc(lo_done, 1)

            def split_low(c, count):
                if count > GROUP and count % GROUP == 0:
                    with dve.Fori(0, count // GROUP) as g:
                        split_group(c, g)
                elif count == GROUP:
                    split_group(c, 0)
                else:
                    for j in range(count):
                        s = slot(c + j)
                        dve.wait_ge(hi_done, c + j + 1)
                        dve.tensor_tensor(w_lo[:, s, :], raw[:, s, :], w_hi[:, s, :].bitcast(F32),
                                          ALU.subtract).then_inc(lo_done, 1)

            def low(t, dst_hi, dst_lo, src):
                dve.wait_ge(tile_hi, t + 1)
                dve.tensor_tensor(dst_lo, src, dst_hi.bitcast(F32), ALU.subtract).then_inc(tile_lo, 1)

            def tiles2(dst, j):
                return dst[:, 2 * j * S:2 * (j + 1) * S]

            def place_free(t):
                dve.wait_ge(tile_lo, t - 1)

            split_low(first["kv", 0], GROUP)
            for g, t in enumerate(use["mem_t"]):
                low(tile["mem_t"] + g, tiles2(c_hi, g), tiles2(c_lo, g), psum[:, t.bank, :])
            split_low(first["kv", 0] + GROUP, KT - GROUP)
            split_low(first["kv", 1], KT)
            split_low(first["qi", 0], GROUP)
            for g, t in enumerate(use["x_t"]):
                low(tile["x_t"] + g, tiles2(x_hi, g), tiles2(x_lo, g), psum[:, t.bank, :])
            dve.wait_ge(tables_ready, 1)
            step(dve.tensor_scalar(tables[:, 1, :], tables[:, 1, :], cst[:, C_SIGN_Q:C_SIGN_Q + 1], None, ALU.mult))
            step(dve.tensor_scalar(tables[:, 3, :], tables[:, 3, :], cst[:, C_SIGN_I:C_SIGN_I + 1], None, ALU.mult))

            def rope(area, rows, t, half):
                heads = area.shape[1]
                mask = list(range(half, 2 * half)) + list(range(half)) + list(range(2 * half, 32))
                tmp = rope_tmp[0:rows, 0:heads * S].rearrange("p (h s) -> p h s", h=heads)
                cos = tables[0:rows, 2 * t:2 * t + 1, :].to_broadcast([rows, heads, S])
                sin = tables[0:rows, 2 * t + 1:2 * t + 2, :].to_broadcast([rows, heads, S])
                step(dve.stream_shuffle(tmp, area, mask))
                step(dve.tensor_tensor(tmp, tmp, sin, ALU.mult))
                step(dve.tensor_tensor(area, area, cos, ALU.mult))
                dve.tensor_tensor(area, area, tmp, ALU.add).then_inc(rope_done, 1)

            def probabilities(h, ready, z, blocks):
                step(dve.reciprocal(rec[:, h, :], sums[:, h, :]))
                for b in range(TB):
                    ins = dve.tensor_scalar(blocks[b], blocks[b], rec[:, h, b:b + 1], None, ALU.mult)
                    if b == 0:
                        step(ins)
                    else:
                        ins.then_inc(probs_ready, 1)

            def add_to_x(tenants, c, stats_too, value=None):
                for b, t in enumerate(tenants):
                    tb, chunk = b // 2, 2 * c + b % 2
                    part = x[:, tb, chunk * 512:(chunk + 1) * 512]
                    dve.tensor_tensor(part, psum[:, t.bank, :], part, ALU.add).then_inc(dve_drained, 1)
                    if stats_too:
                        dve.wait_ge(dve_drained, t.drain[1])
                        step(dve.bn_stats(stats[:, tb, chunk, :], part))

            def normalize(i):
                for b in range(TB):
                    step(dve.bn_aggr(mv[:, b, :], stats[:, b, :, :].rearrange("p c n -> p (c n)")))
                dve.tensor_scalar(var, mv[:, :, 1], EPS, None, ALU.add).then_inc(variance_ready, 1)
                dve.wait_ge(deviation_ready, i + 1)
                step(dve.reciprocal(rstd, dev))
                for b in range(TB):
                    dve.tensor_scalar(x[:, b, :], x[:, b, :], mv[:, b, 0:1], rstd[:, b:b + 1],
                                      ALU.subtract, ALU.mult).then_inc(normalized, 1)

            def norm_tiles(L, i):
                def low_part(j):
                    k = tile["ln_t", L, i] + j
                    low(k, x_hi[:, j * S:(j + 1) * S], x_lo[:, j * S:(j + 1) * S], stage[:, k % 2, 0:S])

                for j in range(KT):
                    t = use["ln_t", L, i][j // 2]
                    k = tile["ln_t", L, i] + j
                    place_free(k)
                    dve.wait_ge(matmuls_done, t.full)
                    v = (3 * L + i) * KT + j
                    dve.tensor_scalar(stage[:, k % 2, 0:S], psum[:, t.bank, (j % 2) * S:(j % 2 + 1) * S],
                                      vec[:, V_G + v:V_G + v + 1], vec[:, V_B + v:V_B + v + 1],
                                      ALU.mult, ALU.add).then_inc(tile_staged, 1)
                    if j > 0:
                        low_part(j - 1)
                low_part(KT - 1)

            def head_logits(L, h):
                t = use["z", L][h]
                dve.wait_ge(matmuls_done, t.full)
                if h >= 2:
                    dve.wait_ge(matmuls_done, use["pt", L][h - 2].full)
                z, ps = probs[:, h % 2, 0:P + S], psum[:, t.bank, 0:P + S]
                if L == 0:
                    ins = dve.scalar_tensor_tensor(out=z, in0=ps, scalar=1.0, in1=score,
                                                   op0=ALU.mult, op1=ALU.add)
                else:
                    step(dve.scalar_tensor_tensor(out=z[:, 0:P], in0=ps[:, 0:P], scalar=decay_tok[:, 0, h:h + 1],
                                                  in1=causal[:, 0:P], op0=ALU.add, op1=ALU.add))
                    ins = dve.scalar_tensor_tensor(out=z[:, P:P + S], in0=ps[:, P:P + S],
                                                   scalar=decay_tok[:, 1, h:h + 1],
                                                   in1=causal[:, P:P + S], op0=ALU.add, op1=ALU.add)
                ins.then_inc(dve_drained, 1)
                dve.wait_ge(dve_drained, t.drain[1])
                for b in range(TB):
                    step(dve.tensor_reduce(neg_max[:, h, b:b + 1], z[:, 0:P] if b == 0 else z[:, P:P + S], AX, ALU.max))
                dve.tensor_scalar(neg_max[:, h, :], neg_max[:, h, :], -SCALE, None, ALU.mult).then_inc(maxima_ready, 1)

            def head_probs(L, h):
                dve.wait_ge(exp_done, L * (2 * HEADS + XHEADS) + 2 * (h + 1))
                z = probs[:, h % 2, :]
                probabilities(h, None, z, (z[:, 0:P], z[:, P:P + S]))

            causal = bias[:, 0, :]

            for L in range(DEPTH):
                if L == 0:
                    split_low(first["qi", L] + GROUP, KT - GROUP)
                    split_low(first["kw"], 2)
                    dve.wait_ge(zeroed, 1)
                    for b, t in enumerate(use["qi", L]):
                        dve.wait_ge(act_drained, t.drain[1])
                        rope(qi_sb[:, 2 * b:2 * b + 2, :], P, 1, 8)
                        dve.wait_ge(rope_done, b + 1)
                    dve.wait_ge(act_drained, use["kw"][0].drain[1])
                    rope(ki[:, :].unsqueeze(1), P, 1, 8)
                    t = use["wi_t"]
                    dve.wait_ge(matmuls_done, t.full)
                    dve.tensor_scalar(wi_tok, psum[:, t.bank, 0:TB * IDX_HEADS].rearrange("p (b h) -> p b h", b=TB),
                                      IDX_HEADS ** -0.5, None, ALU.mult).then_inc(dve_drained, 1)
                    dve.wait_ge(dve_drained, t.drain[1])
                    for i, (_, t) in enumerate(use["idx"]):
                        dve.wait_ge(act_drained, t.drain[1])
                        tb, width = i % TB, P * (i % TB + 1)
                        acc = score[:, 0:P] if tb == 0 else score[:, P:P + S]
                        for j in range(2):
                            h = 2 * (i // TB) + j
                            base = acc if h else cst[:, C_ADMIT + tb * P:C_ADMIT + tb * P + width]
                            ins = dve.scalar_tensor_tensor(
                                out=acc, in0=relu[:, i % 2, j * width:(j + 1) * width],
                                scalar=wi_tok[:, tb, h:h + 1], in1=base, op0=ALU.mult, op1=ALU.add)
                            if j == 0:
                                step(ins)
                            else:
                                ins.then_inc(index_summed, 1)
                                dve.wait_ge(index_summed, i + 1)
                    for b, t in enumerate(use["q", L]):
                        dve.wait_ge(act_drained, t.drain[1])
                        rope(q_sb[0:32, 2 * b:2 * b + 2, :], 32, 0, 16)
                        dve.wait_ge(rope_done, 5 + b + 1)
                    for r in range(TOPK // 8):
                        for tb in range(TB):
                            rows = slice(0, P) if tb == 0 else slice(P, P + S)
                            src = score if r == 0 else work
                            step(dve.max(top8[:, tb, :], src[:, rows]))
                            step(dve.match_replace(work[:, rows], top8[:, tb, :], src[:, rows], TAKEN))
                    dve.tensor_scalar(score, work, (TAKEN + NOT_ADMITTED) / 2, MASKED,
                                      ALU.is_gt, ALU.mult).then_inc(mask_ready, 1)
                    for b, t in enumerate(use["k", L]):
                        dve.wait_ge(act_drained, t.drain[1])
                        rope(k_sb[0:32, 2 * b:2 * b + 2, :], 32, 0, 16)
                        dve.wait_ge(rope_done, 9 + b + 1)
                    dve.wait_ge(mask_ready, 1)
                else:
                    split_low(first["q", L] + GROUP, KT - GROUP)
                    split_low(first["k", L], KT)
                    split_low(first["v", L], KT)
                    split_low(first["f"], 1)
                    step(dve.memset(causal[:, P:S], 0.0))
                    step(dve.tensor_copy(causal[:, 0:P], cst[:, C_TRI:C_TRI + P]))
                    step(dve.tensor_copy(causal[:, S:P + S], cst[:, C_TRI:C_TRI + P]))
                    step(dve.memset(ones8, 1.0))
                    t = use["f"][0]
                    dve.wait_ge(panels_used, first["f"] + 1)
                    ps = psum[0:HEADS, t.bank, 0:S]
                    dve.tensor_scalar(decay, ps, vec[0:HEADS, V_FB:V_FB + 1], None, ALU.add).then_inc(dve_drained, 1)
                    dve.wait_ge(dve_drained, t.drain[1])
                    step(dve.tensor_scalar(dtmp, decay, 0.0, 2.0, ALU.max, ALU.mult))
                    dve.tensor_tensor(dtmp, dtmp, decay, ALU.subtract).then_inc(decay_in, 1)
                    dve.wait_ge(decay_in, 1)
                    step(dve.tensor_scalar(decay, decay, 0.0, None, ALU.min))
                    dve.wait_ge(decay_log, 1)
                    step(dve.tensor_tensor(decay, decay, dtmp, ALU.subtract))
                    step(dve.tensor_scalar(neg_decay, decay, -1.0 / SCALE, None, ALU.mult))
                    step(dve.tensor_tensor_scan(dtmp, ones8, neg_decay, 0.0, ALU.mult, ALU.add))
                    step(dve.tensor_copy(neg_decay, dtmp))
                    dve.tensor_scalar(decay, dtmp, -1.0, None, ALU.mult).then_inc(decay_ready, 1)
                    t = use["ft"]
                    dve.wait_ge(matmuls_done, t.full)
                    dve.tensor_copy(decay_tok, psum[:, t.bank, 0:TB * HEADS].rearrange(
                        "p (b h) -> p b h", b=TB)).then_inc(dve_drained, 1)
                    dve.wait_ge(dve_drained, t.drain[1])

                for h in range(HEADS + 1):
                    if h < HEADS:
                        head_logits(L, h)
                        head_probs(L, h)
                    if h > 0:
                        t = use["o", L][h - 1]
                        j = HEADS + h - 1
                        low(tile["o", L] + h - 1, c_hi[:, j * S:(j + 1) * S], c_lo[:, j * S:(j + 1) * S],
                            psum[:, t.bank, 0:S])
                    if L == 1 and h == HEADS - 1:
                        dve.wait_ge(panels_used, first["gc", L] + KT)
                        for b, t in enumerate(use["gc", L]):
                            dve.wait_ge(act_drained, use["u", L][b].drain[1])
                            u = area_a[:, 2 * b:2 * b + 2, PAD:PW]
                            dve.tensor_tensor(u, psum[:, t.bank, :].rearrange("p (h s) -> p h s", h=2), u,
                                              ALU.mult).then_inc(dve_drained, 1)
                split_from = first["out", L, 0]
                if L == 0:
                    dve.wait_ge(lo_done, split_from)
                    split_low(split_from, 2 * GROUP)
                    for z in (ping, pong):
                        step(dve.memset(z[:, :, 0:PAD], 0.0))
                    dve.wait_ge(act_drained, use["u", L][-1].drain[1])
                    for g, window in enumerate(WINDOWS):
                        u = area_a[:, 2 * g:2 * g + 2, :]
                        src, dst, shift = u, ping, 1
                        while shift < window:
                            step(dve.tensor_tensor(dst[:, :, PAD:PW], src[:, :, PAD:PW],
                                                   src[:, :, PAD - shift:PW - shift], ALU.add))
                            src, dst, shift = dst, (pong if dst is ping else ping), 2 * shift
                        inv = cst[:, C_INVC + g * PAD:C_INVC + g * PAD + window].unsqueeze(1).to_broadcast(
                            [P, 2, window])
                        step(dve.tensor_tensor(src[:, :, PAD:PAD + window], src[:, :, PAD:PAD + window], inv, ALU.mult))
                        dve.scalar_tensor_tensor(out=u[:, :, PAD:PW], in0=src[:, :, PAD:PW],
                                                 scalar=1.0 / window, in1=u[:, :, PAD:PW],
                                                 op0=ALU.mult, op1=ALU.subtract).then_inc(pooled, 1)
                        dve.wait_ge(pooled, g + 1)
                    for g, t in enumerate(use["pool"]):
                        k = tile["branch", L] + g
                        place_free(k)
                        dve.wait_ge(matmuls_done, t.full)
                        for j in range(2):
                            v = V_SCALE + 2 * g + j
                            ins = dve.tensor_scalar(stage[:, k % 2, j * S:(j + 1) * S],
                                                    psum[:, t.bank, j * S:(j + 1) * S],
                                                    vec[:, v:v + 1], None, ALU.mult)
                            if j == 0:
                                step(ins)
                            else:
                                ins.then_inc(tile_staged, 1)
                        low(k, tiles2(c_hi, g), tiles2(c_lo, g), stage[:, k % 2, :])
                else:
                    dve.wait_ge(dve_drained, use["gc", L][-1].drain[1])
                    for j in range(HALF // P):
                        w = [vec[:, V_CONV + 3 * j + i:V_CONV + 3 * j + i + 1] for i in range(3)]
                        y = area_b[:, j, :]
                        step(dve.tensor_scalar(y, area_a[:, j, PAD:PW], w[2], None, ALU.mult))
                        for i in (1, 0):
                            step(dve.scalar_tensor_tensor(out=y, in0=area_a[:, j, PAD - 2 + i:PW - 2 + i],
                                                          scalar=w[i], in1=y, op0=ALU.mult, op1=ALU.add))
                    dve.wait_ge(lo_done, split_from)
                    split_low(split_from, GROUP)
                    dve.wait_ge(panels_used, first["gb", L] + KT)
                    for b, t in enumerate(use["gb", L]):
                        k = tile["branch", L] + b
                        place_free(k)
                        dve.tensor_tensor(stage[:, k % 2, :], psum[:, t.bank, :],
                                          area_b[:, 2 * b:2 * b + 2, :].rearrange("p h s -> p (h s)"),
                                          ALU.mult).then_inc(tile_staged, 1)
                        low(k, tiles2(c_hi, b), tiles2(c_lo, b), stage[:, k % 2, :])
                    split_low(split_from + GROUP, GROUP)
                split_low(split_from + 2 * GROUP, 2 * GROUP)
                split_low(first["out", L, 1], GROUP)
                dve.wait_ge(panels_used, first["out", L, 0] + KT)
                dve.wait_ge(affine_done, 3 * L + 1)
                add_to_x(use["out", L, 0], 0, True)
                split_low(first["out", L, 1] + GROUP, KT - GROUP)
                split_low(first["xq", L], GROUP)
                dve.wait_ge(panels_used, first["out", L, 1] + KT)
                add_to_x(use["out", L, 1], 1, True)
                normalize(3 * L)
                norm_tiles(L, 0)
                split_low(first["xq", L] + GROUP, GROUP)
                split_low(first["xout", L, 0], GROUP)

                for h, t in enumerate(use["xz", L]):
                    dve.wait_ge(matmuls_done, t.full)
                    step(dve.tensor_reduce(neg_max[:, HEADS + h, :], psum[:, t.bank, :].rearrange(
                        "p (b n) -> p b n", b=TB), AX, ALU.max))
                    dve.tensor_scalar(neg_max[:, HEADS + h, :], neg_max[:, HEADS + h, :], -SCALE, None,
                                      ALU.mult).then_inc(maxima_ready, 1)
                for h, t in enumerate(use["xz", L]):
                    dve.wait_ge(exp_done, L * (2 * HEADS + XHEADS) + 2 * HEADS + h + 1)
                    dve.wait_ge(act_drained, t.drain[1])
                    z = xprobs(h)
                    probabilities(HEADS + h, None, z, (z[:, 0, :], z[:, 1, :]))
                for h, t in enumerate(use["xo", L]):
                    low(tile["xo", L] + h, c_hi[:, h * S:(h + 1) * S], c_lo[:, h * S:(h + 1) * S],
                        psum[:, t.bank, 0:S])
                split_low(first["xout", L, 1], GROUP)
                dve.wait_ge(panels_used, first["xout", L, 0] + XHEADS)
                dve.wait_ge(affine_done, 3 * L + 2)
                add_to_x(use["xout", L, 0], 0, True)
                split_low(first["in", L, 0, 0], GROUP)
                dve.wait_ge(panels_used, first["xout", L, 1] + XHEADS)
                add_to_x(use["xout", L, 1], 1, True)
                normalize(3 * L + 1)
                norm_tiles(L, 1)

                def ffn_part(i, units, reg):
                    laps = 0 if reg is None else reg * (first["stride"] // GROUP)

                    def split(c, count):
                        if count > GROUP:
                            with dve.Fori(0, count // GROUP) as g:
                                split_group(c, g if reg is None else g + laps)
                        elif count:
                            split_group(c, laps)

                    def count(value, per_part):
                        return value if reg is None else reg * per_part + value

                    def add_down(c):
                        dve.wait_ge(panels_used, count(first["down", L, i, c] + units * GROUP, first["stride"]))
                        if c == 0:
                            dve.wait_ge(affine_done, 3 * L + 3)
                        for b, t in enumerate(use["down", L, i, c]):
                            tb, chunk = b // 2, 2 * c + b % 2
                            part = x[:, tb, chunk * 512:(chunk + 1) * 512]
                            dve.tensor_tensor(part, psum[:, t.bank, :], part, ALU.add).then_inc(dve_drained, 1)
                            if reg is None:
                                dve.wait_ge(dve_drained, t.drain[1])
                                step(dve.bn_stats(stats[:, tb, chunk, :], part))

                    for j in range(units):
                        c0 = first["in", L, i, j]
                        split(c0 + GROUP, KT - GROUP)
                        after = first["in", L, i, j + 1] if j + 1 < units else first["down", L, i, 0]
                        split(after, GROUP)
                        tenants = use["in", L, i, j]
                        dve.wait_ge(panels_used, count(c0 + KT, first["stride"]))
                        for b in range(2):
                            k = tile["in", L, i, j] + b
                            dve.wait_ge(tile_lo, count(k - 1, stride["lo"]))
                            dve.wait_ge(act_drained, count(tenants[b].drain[1], stride["act"]))
                            dve.tensor_tensor(stage[:, k % 2, :], psum[:, tenants[2 + b].bank, :], gate[:, b, :],
                                              ALU.mult).then_inc(tile_staged, 1)
                        for b in range(2):
                            k = tile["in", L, i, j] + b
                            dst = 2 * j + b
                            dve.wait_ge(tile_hi, count(k + 1, stride["lo"]))
                            dve.tensor_tensor(tiles2(c_lo, dst), stage[:, k % 2, :],
                                              tiles2(c_hi, dst).bitcast(F32), ALU.subtract).then_inc(tile_lo, 1)
                    for c in range(2):
                        c0 = first["down", L, i, c]
                        split(c0 + GROUP, (units - 1) * GROUP)
                        if c == 0:
                            split(first["down", L, i, 1], GROUP)
                            add_down(0)
                        elif i < PARTS:
                            split(c0 + units * GROUP, GROUP)
                            add_down(1)

                with dve.Fori(0, PARTS) as i:
                    ffn_part(0, PART_UNITS, i)
                ffn_part(PARTS, LAST_UNITS, None)
                if L < DEPTH - 1:
                    split_low(first["q", L + 1], GROUP)
                c0 = first["down", L, PARTS, 1]
                dve.wait_ge(panels_used, c0 + LAST_UNITS * GROUP)
                add_to_x(use["down", L, PARTS, 1], 1, True)
                normalize(3 * L + 2)
                if L < DEPTH - 1:
                    norm_tiles(L, 2)
            dve.wait_ge(gain_in, 32 * 3 * DEPTH)
            for b in range(TB):
                dve.wait_ge(normalized, TB * 3 * (DEPTH - 1) + 2 * TB + b + 1)
                step(dve.tensor_tensor(x[:, b, :], x[:, b, :], gain, ALU.mult))
                dve.tensor_tensor(x[:, b, :], x[:, b, :], offset, ALU.add).then_inc(affine_done, 1)

        @block.tensor
        def _(pe):
            def passes(pairs, out, start, stop=False):
                (lh, ll), (rh, rl) = pairs
                pe.matmul(out, lh, rh, start=start, stop=False, skip_group_check=True)
                pe.matmul(out, lh, rl, start=False, stop=False, skip_group_check=True)
                return pe.matmul(out, ll, rh, start=False, stop=stop, skip_group_check=True)

            def weight(s, lo_col, width):
                return w_hi[:, s, lo_col:lo_col + width], w_lo[:, s, lo_col:lo_col + width]

            def activations(kind, t, lo_col=0, width=S):
                hi, lo = (x_hi, x_lo) if kind == "x" else (c_hi, c_lo)
                if isinstance(t, int):
                    return hi[:, t * S + lo_col:t * S + lo_col + width], lo[:, t * S + lo_col:t * S + lo_col + width]
                return hi[:, bass.ds(t * S + lo_col, width)], lo[:, bass.ds(t * S + lo_col, width)]

            def panel_split(c, laps=0):
                pe.wait_ge(lo_done, later(c + 1, laps, GROUP))

            def feature_major(c, laps, tenants, kind, t, opening, cols=0, tiles=8, reg=None, last=True):
                s = slot(c)
                act_pair = activations(kind, t)
                for j in range(tiles):
                    tenant = tenants[j // 2]
                    if opening and j % 2 == 0:
                        wait_drained(pe, tenant, reg)
                    ins = passes((weight(s, cols + j * P, P), act_pair),
                                 psum[:, tenant.bank, (j % 2) * S:(j % 2 + 1) * S], opening and j % 2 == 0)
                if last:
                    ins.then_inc(panels_used, 1)

            def token_major(c, laps, tenants, kind, t, opening, cols=0, chunks=2, reg=None):
                s = slot(c)
                for b in range(TB):
                    stationary = activations(kind, t, b * P, P)
                    for j in range(chunks):
                        tenant = tenants[chunks * b + j]
                        if opening:
                            wait_drained(pe, tenant, reg)
                        (xh, xl), (wh, wl) = stationary, weight(s, cols + j * 512, 512)
                        out = psum[:, tenant.bank, :]
                        pe.matmul(out, xh, wh, start=opening, stop=False, skip_group_check=True)
                        pe.matmul(out, xh, wl, start=False, stop=False, skip_group_check=True)
                        ins = pe.matmul(out, xl, wh, start=False, stop=False, skip_group_check=True)
                ins.then_inc(panels_used, 1)

            def unit(name, key, kind="x"):
                c0 = first[name]
                for j in range(GROUP):
                    panel_split(c0 + j)
                    feature_major(c0 + j, 0, use[key], kind, j, j == 0)
                with pe.Fori(1, KT // GROUP) as g:
                    for j in range(GROUP):
                        panel_split(c0 + j, g)
                        feature_major(c0 + j, g, use[key], kind, g * GROUP + j, False)

            def unit_token_major(key, order, kind):
                c0 = first[key]
                for j, t in enumerate(order):
                    panel_split(c0 + j)
                    token_major(c0 + j, 0, use[key], kind, t, j == 0)

            def transposes(tenant, g, src):
                wait_drained(pe, tenant)
                for j in range(2):
                    for b in range(TB):
                        col = j * S + b * P
                        t = 2 * g + j
                        ins = pe.matmul(psum[:, tenant.bank, col:col + P], src[:, b, t * P:(t + 1) * P], ident,
                                        start=(j == 0 and b == 0), stop=True, is_transpose=True,
                                        skip_group_check=True)
                ins.then_inc(matmuls_done, 1)

            def transposed_unit(name, batch, panel, tiles_per_batch, src, per_panel=1, count=KT):
                for g in range(4):
                    transposes(use[name][g], g, src)
                g = 4
                for j in range(count):
                    t = (j + 1) * per_panel - 1
                    pe.wait_ge(tile_lo, tile[name] + t // tiles_per_batch + 1)
                    panel(j)
                    if g < KT // 2:
                        transposes(use[name][g], g, src)
                        g += 1

            def kv_panel(L):
                def run(j):
                    c = first["kv", L] + j
                    panel_split(c)
                    tenants = use["kv", L]
                    feature_major(c, 0, tenants[0:2], "c", j, j == 0, 0, 4, last=False)
                    token_major(c, 0, tenants[2:4], "c", j, j == 0, XW, 1)
                return run

            pe.wait_ge(consts_in, 16)
            pe.wait_ge(mem_arrived, 16 * TB)
            transposed_unit("mem_t", None, kv_panel(0), 2, mem_tok)
            for j in range(KT):
                kv_panel(1)(j)

            def unit_panel(key, kind="x"):
                def run(j):
                    panel_split(first[key] + j)
                    feature_major(first[key] + j, 0, use[key], kind, j, j == 0)
                return run

            def scores(L, h, t):
                wait_drained(pe, t)
                ps = psum[:, t.bank, :]
                for b, cols in ((0, (0, P)), (1, (P, P + S))):
                    width = cols[1] - cols[0]
                    ins = pe.matmul(ps[:, cols[0]:cols[1]], q_sb[:, h, b * P:(b + 1) * P], k_sb[:, h, 0:width],
                                    start=(b == 0), stop=(L == 0), skip_group_check=True)
                    if L == 1:
                        ins = pe.matmul(ps[:, cols[0]:cols[1]],
                                        ident[0:HEADS, h:h + 1].to_broadcast([HEADS, P]),
                                        neg_decay[:, 0:width], start=False, stop=True, skip_group_check=True)
                ins.then_inc(matmuls_done, 1)

            def transpose_probs(L, h, t):
                pe.wait_ge(probs_ready, L * (HEADS + XHEADS) + h + 1)
                wait_drained(pe, t)
                for j in range(3):
                    ins = pe.matmul(psum[:, t.bank, j * P:(j + 1) * P], probs[:, h % 2, j * P:(j + 1) * P], ident,
                                    start=(j == 0), stop=True, is_transpose=True, skip_group_check=True)
                ins.then_inc(matmuls_done, 1)

            def weighted_values(L, h, t):
                pe.wait_ge(act_drained, use["pt", L][h].drain[1])
                wait_drained(pe, t)
                pt = probs_t[:, h % 2, :]
                pe.matmul(psum[:, t.bank, 0:S], v_sb[:, 0, h * HD:(h + 1) * HD], pt[:, 0:S],
                          start=True, stop=False, skip_group_check=True)
                pe.matmul(psum[:, t.bank, P:S], v_sb[:, 1, h * HD:(h + 1) * HD], pt[:, S:S + P],
                          start=False, stop=True, skip_group_check=True).then_inc(matmuls_done, 1)

            pe.wait_ge(x_arrived, 16 * TB)
            transposed_unit("x_t", None, unit_panel(("qi", 0)), 2, x)
            for L in range(DEPTH):
                if L == 0:
                    t = use["kw"][0]
                    wide = IDX_DIM + IDX_HEADS
                    for j in range(KT):
                        c = first["kw"] + j // 8
                        if j % 8 == 0:
                            panel_split(c)
                        if j == 0:
                            wait_drained(pe, t)
                        ins = passes((weight(slot(c), (j % 8) * wide, wide), activations("x", j)),
                                     psum[0:wide, t.bank, 0:S], j == 0)
                        if j % 8 == 7:
                            ins.then_inc(panels_used, 1)
                    unit(("q", L), ("q", L))
                    t = use["wi_t"]
                    pe.wait_ge(act_drained, use["kw"][0].drain[1])
                    wait_drained(pe, t)
                    rows = slice(IDX_DIM, IDX_DIM + IDX_HEADS)
                    for b in range(TB):
                        ins = pe.matmul(psum[:, t.bank, b * IDX_HEADS:(b + 1) * IDX_HEADS],
                                        tall[rows, 0, b * P:(b + 1) * P], ident[rows, rows],
                                        start=(b == 0), stop=True, is_transpose=True, skip_group_check=True)
                    ins.then_inc(matmuls_done, 1)
                    pe.wait_ge(rope_done, 5)
                    for i, pair in enumerate(use["idx"]):
                        tb = i % TB
                        width = P * (tb + 1)
                        for j in range(2):
                            rows = slice(j * IDX_DIM, (j + 1) * IDX_DIM)
                            wait_drained(pe, pair[j])
                            ins = pe.matmul(psum[:, pair[j].bank, 0:width],
                                            qi_sb[rows, i // TB, tb * P:(tb + 1) * P], ki[rows, 0:width],
                                            start=True, stop=True)
                        ins.then_inc(matmuls_done, 1)
                    unit(("k", L), ("k", L))
                    unit_token_major(("v", L), range(KT), "x")
                    pe.wait_ge(rope_done, 13)
                else:
                    transposed_unit(("ln_t", L - 1, 2), None, unit_panel(("q", L)), 1, x)
                    unit(("k", L), ("k", L))
                    unit_token_major(("v", L), range(KT), "x")
                    t = use["f"][0]
                    panel_split(first["f"])
                    wait_drained(pe, t)
                    for j in range(KT):
                        ins = passes((weight(slot(first["f"]), j * HEADS, HEADS), activations("x", j)),
                                     psum[0:HEADS, t.bank, 0:S], j == 0)
                    ins.then_inc(panels_used, 1)
                    panels_between = iter(range(3 * KT))
                    t = use["ft"]
                    wait_drained(pe, t)
                    pe.wait_ge(decay_ready, 1)
                    for b in range(TB):
                        ins = pe.matmul(psum[:, t.bank, b * HEADS:(b + 1) * HEADS], decay[:, b * P:(b + 1) * P],
                                        ident[0:HEADS, 0:HEADS], start=(b == 0), stop=True, is_transpose=True,
                                        skip_group_check=True)
                    ins.then_inc(matmuls_done, 1)
                    pe.wait_ge(act_drained, use["k", L][-1].drain[1])
                fills = [unit_panel(("u", L))] * KT + ([unit_panel(("gc", L))] * KT if L else [])
                fills = [(f, j % KT) for j, f in enumerate(fills)]
                per_head = len(fills) // HEADS
                for h in range(HEADS + 1):
                    if h < HEADS:
                        scores(L, h, use["z", L][h])
                    if h > 0:
                        transpose_probs(L, h - 1, use["pt", L][h - 1])
                    for i in range(per_head if h < HEADS else 0):
                        if i == per_head // 2 and h > 0:
                            if h == 1:
                                pe.wait_ge(act_drained, use["v", L][-1].drain[1])
                            weighted_values(L, h - 1, use["o", L][h - 1])
                        run, j = fills[h * per_head + i]
                        run(j)
                weighted_values(L, HEADS - 1, use["o", L][HEADS - 1])
                if L == 1:
                    unit(("gb", L), ("gb", L))
                order = attention_order(L)
                for c in range(2):
                    key = ("out", L, c)
                    for j, t in enumerate(order):
                        if c == 0 and j < HEADS:
                            pe.wait_ge(tile_lo, tile["o", L] + j + 1)
                        if c == 0 and j >= HEADS:
                            if L == 0 and j == HEADS:
                                pe.wait_ge(pool_w_in, 16)
                                pw = area_b[:, :, :].rearrange("p h s -> p (h s)").rearrange(
                                    "p (g t d) -> p g t d", g=GROUPS, t=2)
                                for g, tenant in enumerate(use["pool"]):
                                    wait_drained(pe, tenant)
                                    pe.wait_ge(pooled, g + 1)
                                    for d in range(2):
                                        for i in range(2):
                                            ins = pe.matmul(psum[:, tenant.bank, d * S:(d + 1) * S],
                                                            pw[:, g, i, d * P:(d + 1) * P],
                                                            area_a[:, 2 * g + i, PAD:PW],
                                                            start=(d == 0 and i == 0), stop=(i == 1),
                                                            skip_group_check=True)
                                    ins.then_inc(matmuls_done, 1)
                            pe.wait_ge(tile_lo, tile["branch", L] + (j - HEADS) // 2 + 1)
                        panel_split(first[key] + j)
                        token_major(first[key] + j, 0, use[key], "c", t, j == 0)

                def xq_panel(j):
                    c = first["xq", L] + j
                    panel_split(c)
                    for i in range(2):
                        feature_major(c, 0, use["xq", L], "x", 2 * j + i, j == 0 and i == 0, i * XW, 4, last=(i == 1))

                pe.wait_ge(normalized, TB * (3 * L + 1))
                transposed_unit(("ln_t", L, 0), None, xq_panel, 1, x, 2, KT // 2)
                pe.wait_ge(act_drained, use["xq", L][-1].drain[1])
                for h, t in enumerate(use["xz", L]):
                    wait_drained(pe, t)
                    for b in range(TB):
                        ins = pe.matmul(psum[:, t.bank, b * S:(b + 1) * S], q_sb[:, h, b * P:(b + 1) * P],
                                        k_mem[:, L, h, :], start=(b == 0), stop=True, skip_group_check=True)
                    ins.then_inc(matmuls_done, 1)
                for h in range(XHEADS + 1):
                    if h < XHEADS:
                        t = use["xpt", L][h]
                        pe.wait_ge(probs_ready, L * (HEADS + XHEADS) + HEADS + h + 1)
                        wait_drained(pe, t)
                        for m in range(2):
                            for b in range(TB):
                                col = m * S + b * P
                                ins = pe.matmul(psum[:, t.bank, col:col + P], xprobs(h)[:, b, m * P:(m + 1) * P],
                                                ident, start=(m == 0 and b == 0), stop=True, is_transpose=True,
                                                skip_group_check=True)
                        ins.then_inc(matmuls_done, 1)
                    if h > 0:
                        t = use["xo", L][h - 1]
                        pe.wait_ge(act_drained, use["xpt", L][h - 1].drain[1])
                        wait_drained(pe, t)
                        for m in range(2):
                            ins = pe.matmul(psum[:, t.bank, 0:S], v_mem[:, L, m, (h - 1) * HD:h * HD],
                                            xprobs_t(h - 1)[:, m * S:(m + 1) * S],
                                            start=(m == 0), stop=(m == 1), skip_group_check=True)
                        ins.then_inc(matmuls_done, 1)
                for c in range(2):
                    for j in range(XHEADS):
                        pe.wait_ge(tile_lo, tile["xo", L] + j + 1)
                        panel_split(first["xout", L, c] + j)
                        token_major(first["xout", L, c] + j, 0, use["xout", L, c], "c", j, j == 0)
                pe.wait_ge(normalized, TB * (3 * L + 2))

                def ffn_part(i, units, reg, already=False):
                    laps = 0 if reg is None else reg * (first["stride"] // GROUP)
                    for j in range(units):
                        c0 = first["in", L, i, j]
                        for t in range(GROUP):
                            panel_split(c0 + t, laps)
                            feature_major(c0 + t, laps, use["in", L, i, j], "x", t, t == 0, reg=reg)
                        with pe.Fori(1, KT // GROUP) as g:
                            for t in range(GROUP):
                                panel_split(c0 + t, g if reg is None else g + laps)
                                feature_major(c0 + t, 0, use["in", L, i, j], "x", g * GROUP + t, False)
                    for c in range(2):
                        c0 = first["down", L, i, c]
                        for j in range(units * GROUP):
                            if c == 0 and j % 2 == 0:
                                need = tile["in", L, i, j // GROUP] + (j % GROUP) // 2 + 1
                                pe.wait_ge(tile_lo, need if reg is None else reg * stride["lo"] + need)
                            panel_split(c0 + j, laps)
                            token_major(c0 + j, laps, use["down", L, i, c], "c", j, j == 0, reg=reg)

                for g in range(4):
                    transposes(use["ln_t", L, 1][g], g, x)
                for g in range(4, 8):
                    transposes(use["ln_t", L, 1][g], g, x)
                pe.wait_ge(tile_lo, tile["ln_t", L, 1] + KT)
                with pe.Fori(0, PARTS) as i:
                    ffn_part(0, PART_UNITS, i)
                ffn_part(PARTS, LAST_UNITS, None)
                if L < DEPTH - 1:
                    pe.wait_ge(normalized, TB * (3 * L + 3))


def shape_constants():
    c = np.zeros((P, C_END), np.float32)
    c[:, C_ID:C_ID + P] = np.eye(P)
    row = np.arange(P)
    for freq, sign, dim in ((C_FREQ_Q, C_SIGN_Q, HD), (C_FREQ_I, C_SIGN_I, IDX_DIM)):
        rot = dim // 4
        half = rot // 2
        inv = np.power(np.float32(ROPE_THETA), -(np.arange(half, dtype=np.float32) * np.float32(2.0) / np.float32(rot)))
        at = row % dim
        for r in range(P):
            if at[r] < rot:
                c[r, freq] = inv[at[r] % half]
                c[r, sign] = -1.0 if at[r] < half else 1.0
    c[:, C_TRI:C_TRI + P] = np.where(row[None, :] <= row[:, None], 0.0, MASKED)
    t0, s0 = row[:, None], row[None, :]
    c[:, C_ADMIT:C_ADMIT + P] = np.where(s0 // CHUNK <= t0 // CHUNK, 0.0, NOT_ADMITTED)
    s1 = np.arange(S)[None, :]
    c[:, C_ADMIT + P:C_ADMIT + P + S] = np.where(s1 // CHUNK <= (P + t0) // CHUNK, 0.0, NOT_ADMITTED)
    for g, w in enumerate(WINDOWS):
        n = np.arange(PAD) + 1
        c[:, C_INVC + g * PAD:C_INVC + (g + 1) * PAD] = np.where(n < w, w / n, 1.0)
    return c


def kernel(x, mem, positions, ev_w_in, ev_pool_w, ev_pool_scale, ev_w_out, od_w_in, od_conv_w, od_forget_b,
           od_w_out, ca_w_q, ca_w_kv, ca_w_o, ffn_w_in, ffn_w_out, ln_g, ln_b):
    import concourse.bacc as bacc
    from concourse.bass_utils import run_bass_kernel_spmd

    arrays = {n: np.ascontiguousarray(v) for n, v in dict(
        x=x, mem=mem, positions=positions, ev_w_in=ev_w_in, ev_pool_w=ev_pool_w, ev_w_out=ev_w_out,
        od_w_in=od_w_in, od_w_out=od_w_out, ca_w_q=ca_w_q, ca_w_kv=ca_w_kv, ca_w_o=ca_w_o,
        ffn_w_in=ffn_w_in, ffn_w_out=ffn_w_out, ln_g=ln_g, ln_b=ln_b).items()}
    v = np.zeros((P, V_END), np.float32)
    v[:, V_G:V_B] = np.asarray(ln_g).reshape(DEPTH * 3 * KT, P).T
    v[:, V_B:V_SCALE] = np.asarray(ln_b).reshape(DEPTH * 3 * KT, P).T
    v[:, V_SCALE:V_CONV] = np.asarray(ev_pool_scale).reshape(HALF // P, P).T
    v[:, V_CONV:V_FB] = np.asarray(od_conv_w)[0].reshape(3, HALF // P, P).transpose(2, 1, 0).reshape(P, -1)
    v[:HEADS, V_FB] = np.asarray(od_forget_b)[0]
    arrays["vectors"] = v
    arrays["shape_constants"] = shape_constants()

    nc = bacc.Bacc("TRN2", target_bir_lowering=False, num_devices=1)
    aps = {n: nc.dram_tensor(n + "_dram", v.shape, mybir.dt.from_np(v.dtype), kind="ExternalInput").ap()
           for n, v in arrays.items()}
    aps["out"] = nc.dram_tensor("out_dram", (1, S, D), F32, kind="ExternalOutput").ap()
    build(nc, aps)
    r = run_bass_kernel_spmd(nc, [{n + "_dram": v for n, v in arrays.items()}], core_ids=[0])
    return r.results[0]["out_dram"]
```

```python
from contextlib import ExitStack

import concourse.bass as bass
from concourse import mybir
import numpy as np

F32 = mybir.dt.float32
F32R = mybir.dt.float32r
I32 = mybir.dt.int32
ALU = mybir.AluOpType
ACT = mybir.ActivationFunctionType
AX = mybir.AxisListType.X

P = 128
D = 2048
S = 256
TB = S // P
KT = D // P
HALF = D // 2
HD = 128
HEADS = HALF // HD
XHEADS = 4
XW = XHEADS * HD
IDX_HEADS, IDX_DIM = 16, 64
TOPK = 64
CHUNK = 64
GROUPS = 4
WINDOWS = (2, 4, 8, 16)
PAD = 16
PW = PAD + S
DEPTH = 2
FFN = 5632
FU = 512
UNITS = FFN // FU
PART_UNITS = 3
PARTS = UNITS // PART_UNITS
LAST_UNITS = UNITS - PARTS * PART_UNITS
ALPHA = float((2 * DEPTH) ** 0.25)
EPS = 1e-5
SCALE = float(HD) ** -0.5
ROPE_THETA = 500000.0
PANEL = 1024
RAW = 4
SPLIT = 4
CLOSE = 2
CLOSE_LAST = 3
GROUP = 4
NOT_ADMITTED = -2.0e38
TAKEN = -3.0e38
MASKED = -1.0e30
TWO_PI = 2.0 * np.pi

C_ID = 0
C_FREQ_Q, C_SIGN_Q, C_FREQ_I, C_SIGN_I = 128, 129, 130, 131
C_TRI = 132
C_ADMIT = C_TRI + P
C_INVC = C_ADMIT + P + S
C_END = C_INVC + GROUPS * PAD
V_G = 0
V_B = V_G + DEPTH * 3 * KT
V_SCALE = V_B + DEPTH * 3 * KT
V_CONV = V_SCALE + HALF // P
V_FB = V_CONV + 3 * HALF // P
V_END = V_FB + 1


def two_pi_parts():
    a = np.floor(TWO_PI * 2.0 ** 9) / 2.0 ** 9
    b = np.floor((TWO_PI - a) * 2.0 ** 21) / 2.0 ** 21
    return float(a), float(b), float(np.float32(TWO_PI - a - b))


class Tenant:

    def __init__(self, bank, need, drain, full):
        self.bank, self.need, self.drain, self.full = bank, need, drain, full


class Plan:

    def __init__(self):
        self.count = {"act": 0, "dve": 0, "staged": 0, "lo": 0}
        self.last = [None] * 8
        self.matmuls = 0

    def use(self, bank, drainer, times=1, panel=False):
        if not panel:
            self.matmuls += 1
        tenant = Tenant(bank, self.last[bank], None, None if panel else self.matmuls)
        if drainer:
            self.drained(tenant, drainer, times)
        return tenant

    def drained(self, tenant, drainer, times=1):
        self.count[drainer] += times
        tenant.drain = self.last[tenant.bank] = (drainer, self.count[drainer])

    def unit(self, half, drainers=("act",) * 4, closing=True):
        tenants = [self.use(4 * half + b, d, panel=True) for b, d in enumerate(drainers)]
        if closing:
            self.closed(tenants)
        return tenants

    def closed(self, tenants):
        for t in tenants[:-1]:
            self.matmuls += 1
            t.full = self.matmuls


def make_plan():
    p, use, first, tile, staged = Plan(), {}, {}, {}, {}
    at = 0

    def panels(name, count):
        nonlocal at
        first[name] = at
        at += count

    def split_now(name):
        tile[name], staged[name] = p.count["lo"], p.count["staged"]

    def lo(banks):
        return [p.use(b, "lo") for b in banks]

    def norm_tiles(name, half):
        split_now(name)
        use[name] = [p.use(4 * half + g % 4, "staged", times=2) for g in range(KT // 2)]
        p.count["lo"] += KT

    split_now("mem_t")
    use["mem_t"] = lo(g % 4 for g in range(KT // 2))
    use["kv", 0] = p.unit(1, closing=False)
    panels(("kv", 0), KT)
    use["kv", 1] = p.unit(0, closing=False)
    panels(("kv", 1), KT)
    split_now("x_t")
    use["x_t"] = lo(4 + g % 4 for g in range(KT // 2))
    half = 0
    for L in range(DEPTH):
        if L == 0:
            use["qi", L] = p.unit(half)
            panels(("qi", L), KT)
            use["kw"] = [p.use(4 * (1 - half) + 3, "act", panel=True)]
            panels("kw", 2)
            use["q", L] = p.unit(1 - half)
            panels(("q", L), KT)
            use["wi_t"] = p.use(4 * half, "dve")
            use["idx"] = []
            for i in range(IDX_HEADS):
                even = p.use(4 * half + 2 * (i % 2), None, panel=True)
                odd = p.use(4 * half + 2 * (i % 2) + 1, "act")
                p.last[even.bank] = even.drain = odd.drain
                use["idx"].append((even, odd))
            use["k", L] = p.unit(1 - half)
            panels(("k", L), KT)
            use["v", L] = p.unit(half)
            panels(("v", L), KT)
            fill, att = half, 1 - half
        else:
            use["q", L] = p.unit(half)
            panels(("q", L), KT)
            use["k", L] = p.unit(1 - half)
            panels(("k", L), KT)
            use["f"] = [p.use(4 * (1 - half), "dve", panel=True)]
            panels("f", 1)
            use["v", L] = p.unit(half)
            panels(("v", L), KT)
            use["ft"] = p.use(4 * (1 - half) + 1, "dve")
            fill, att = 1 - half, half
        use["z", L], use["pt", L], use["o", L] = [], [], []
        panels(("u", L), KT)
        if L == 1:
            panels(("gc", L), KT)
            panels(("gb", L), KT)
        split_now(("o", L))
        for h in range(HEADS + 1):
            if h == 0:
                use["u", L] = p.unit(fill, (None,) * 4, closing=False)
            if L == 1 and h == HEADS // 2:
                use["gc", L] = p.unit(fill, (None,) * 4, closing=False)
            if h < HEADS:
                use["z", L].append(p.use(4 * att + h % 2, "dve"))
            if h > 0:
                use["pt", L].append(p.use(4 * att + 2, "act"))
            if h == (HEADS if L == 0 else HEADS // 2 - 1):
                for t in use["u", L]:
                    p.drained(t, "act")
            if h > 0:
                use["o", L].append(p.use(4 * att + 3, "lo"))
            if L == 1 and h == HEADS - 1:
                for t in use["gc", L]:
                    p.drained(t, "dve")
        split_now(("branch", L))
        if L == 0:
            use["out", L, 0] = p.unit(att, ("dve",) * 4, closing=False)
            use["pool"] = [p.use(4 * fill + g, "staged") for g in range(GROUPS)]
            p.closed(use["out", L, 0])
        else:
            use["gb", L] = p.unit(fill, ("staged",) * 4)
            use["out", L, 0] = p.unit(att, ("dve",) * 4)
        p.count["lo"] += 4
        panels(("out", L, 0), KT)
        use["out", L, 1] = p.unit(fill, ("dve",) * 4)
        panels(("out", L, 1), KT)
        a, b = att, fill
        norm_tiles(("ln_t", L, 0), a)
        use["xq", L] = [p.use(4 * b + i, "act", panel=True) for i in range(2)]
        p.closed(use["xq", L])
        panels(("xq", L), KT // 2)
        use["xz", L] = [p.use(4 * a + h, None) for h in range(XHEADS)]
        use["xpt", L], use["xo", L] = [], []
        split_now(("xo", L))
        for h in range(XHEADS - 1):
            p.drained(use["xz", L][h], "act")
        for h in range(XHEADS + 1):
            if h < XHEADS:
                use["xpt", L].append(p.use(4 * b + h % 2, "act"))
            if h == 0:
                p.drained(use["xz", L][-1], "act")
            if h > 0:
                use["xo", L].append(p.use(4 * b + 2 + (h - 1) % 2, "lo"))
        use["xout", L, 0] = p.unit(a, ("dve",) * 4)
        panels(("xout", L, 0), XHEADS)
        use["xout", L, 1] = p.unit(b, ("dve",) * 4)
        panels(("xout", L, 1), XHEADS)
        norm_tiles(("ln_t", L, 1), a)
        for i in range(PARTS + 1):
            before = dict(p.count), at, p.matmuls
            s = b
            for j in range(PART_UNITS if i < PARTS else LAST_UNITS):
                split_now(("in", L, i, j))
                use["in", L, i, j] = p.unit(s, ("act", "act", "staged", "staged"), closing=False)
                p.count["lo"] += 2
                panels(("in", L, i, j), KT)
                s = 1 - s
            for c in range(2):
                use["down", L, i, c] = p.unit(s, ("dve",) * 4)
                panels(("down", L, i, c), (PART_UNITS if i < PARTS else LAST_UNITS) * GROUP)
                s = 1 - s
            if i < PARTS:
                use["stride"] = {w: p.count[w] - before[0][w] for w in p.count}
                use["stride"]["matmuls"] = p.matmuls - before[2]
                first["stride"] = at - before[1]
        last = 1 - s
        first["next", L] = at
        if L < DEPTH - 1:
            norm_tiles(("ln_t", L, 2), 1 - last)
        half = last
    for L in range(DEPTH):
        for j in range(PART_UNITS):
            for b, t in enumerate(use["in", L, 0, j]):
                who, value = use["in", L, 1, j][b].need
                t.need = (who, value - use["stride"][who])
        for c in range(2):
            for b, t in enumerate(use["down", L, 0, c]):
                who, value = use["down", L, 1, c][b].need
                t.need = (who, value - use["stride"][who])
    return use, first, tile, staged


def build(nc, a):
    use, first, tile, staged = make_plan()
    stride = use["stride"]
    consts, vectors, pos = a["shape_constants"], a["vectors"], a["positions"]
    x_in, mem_in, out = a["x"], a["mem"], a["out"]
    x_view = x_in.rearrange("o (b p) d -> p (o b) d", p=P)
    mem_view = mem_in.rearrange("o (b p) d -> p (o b) d", p=P)
    out_view = out.rearrange("o (b p) d -> p (o b) d", p=P)
    w_mix = [a["ev_w_in"][0], a["od_w_in"][0]]
    w_out = [a["ev_w_out"][0], a["od_w_out"][0]]
    w_down = a["ffn_w_out"]
    w_up = a["ffn_w_in"].rearrange("l k (g n) -> l k g n", g=2)
    pool_w = a["ev_pool_w"].rearrange("o g (t p) d -> p (o g t) d", p=P)

    with ExitStack() as ctx:
        def sb(name, shape, dt=F32):
            return ctx.enter_context(nc.sbuf_tensor(name, shape, dt))

        def sem(name):
            return ctx.enter_context(nc.semaphore(name))

        raw = sb("raw", [P, RAW, PANEL])
        w_hi = sb("w_hi", [P, SPLIT, PANEL], F32R)
        w_lo = sb("w_lo", [P, SPLIT, PANEL], F32R)
        x = sb("x_tok", [P, TB, D])
        x_hi = sb("x_hi", [P, KT * S], F32R)
        x_lo = sb("x_lo", [P, KT * S], F32R)
        c_hi = sb("c_hi", [P, KT * S], F32R)
        c_lo = sb("c_lo", [P, KT * S], F32R)
        k_mem = sb("k_mem", [P, DEPTH, XHEADS, S])
        v_mem = sb("v_mem", [P, DEPTH, TB, XW])
        area_a = sb("area_a", [P, HALF // P, PW])
        area_b = sb("area_b", [P, HALF // P, S])
        area_cd = sb("area_cd", [P, 2, HALF // P * S])
        stage = sb("stage", [P, 2, 2 * S])
        scratch = sb("scratch", [P, XHEADS * TB * S])
        bias = sb("bias", [P, 2, P + S])
        cst = sb("cst", [P, C_END])
        vec = sb("vec", [P, V_END])
        small = sb("small", [P, 256])
        tall = sb("tall", [P, 4, S])
        ki = sb("ki", [P, S])

        psum = ctx.enter_context(nc.psum_tensor("psum", [P, 8, 512], F32))

        q_sb = area_b
        pool_w_sb = area_b[:, :, :].rearrange("p h s -> p (h s)").rearrange("p (g t d) -> p g t d", g=GROUPS, t=2)
        k_sb = area_cd[:, 0, :].rearrange("p (h s) -> p h s", h=HEADS)
        v_sb = area_cd[:, 1, :].rearrange("p (b n) -> p b n", b=TB)
        qi_sb = area_cd[:, 1, :].rearrange("p (h s) -> p h s", h=HEADS)
        mem_tok = area_cd
        gain, offset = area_cd[:, 0, :], area_cd[:, 1, :]
        ident = cst[:, C_ID:C_ID + P]
        relu = scratch[:, 0:1024].rearrange("p (b n) -> p b n", b=2)
        rope_tmp = scratch[:, 0:512]
        tables = scratch[:, 1024:2048].rearrange("p (t s) -> p t s", t=4)
        probs = scratch[:, 0:1024].rearrange("p (b n) -> p b n", b=2)
        probs_t = scratch[:, 1024:2048].rearrange("p (b n) -> p b n", b=2)
        ping = scratch[:, 0:2 * PW].rearrange("p (t n) -> p t n", t=2)
        pong = scratch[:, 2 * PW:4 * PW].rearrange("p (t n) -> p t n", t=2)
        gate = scratch[:, 0:1024].rearrange("p (b n) -> p b n", b=2)

        def xprobs(h):
            return scratch[:, 512 * h:512 * (h + 1)].rearrange("p (b n) -> p b n", b=TB)

        def xprobs_t(h):
            return area_b[:, 4 + 2 * (h % 2):6 + 2 * (h % 2), :].rearrange("p t n -> p (t n)")

        score, work = bias[:, 0, :], bias[:, 1, :]
        decay, neg_decay = tall[0:HEADS, 0, :], tall[0:HEADS, 1, :]
        dtmp, ones8 = tall[0:HEADS, 2, :], tall[0:HEADS, 3, :]
        wi_tok = small[:, 0:32].rearrange("p (b h) -> p b h", b=TB)
        decay_tok = small[:, 32:48].rearrange("p (b h) -> p b h", b=TB)
        neg_max = small[:, 48:80].rearrange("p (h b) -> p h b", b=TB)
        sums = small[:, 80:112].rearrange("p (h b) -> p h b", b=TB)
        rec = small[:, 112:144].rearrange("p (h b) -> p h b", b=TB)
        top8 = small[:, 144:160].rearrange("p (b n) -> p b n", b=TB)
        stats = small[:, 160:208].rearrange("p (b c n) -> p b c n", b=TB, c=4)
        mv = small[:, 208:212].rearrange("p (b n) -> p b n", b=TB)
        dev, rstd = small[:, 214:216], small[:, 216:218]
        warm, mean_shift, eps = small[:, 218:220], small[:, 220:222], small[:, 222:223]

        ident_in, consts_in = sem("ident_in"), sem("consts_in")
        vectors_in, positions_in = sem("vectors_in"), sem("positions_in")
        x_arrived, mem_arrived = sem("x_arrived"), [sem(f"mem_arrived{i}") for i in range(4)]
        gain_in, pool_w_in, stored = sem("gain_in"), sem("pool_w_in"), sem("stored")
        landed = [sem(f"landed{i}") for i in range(RAW)]
        hi_done, lo_done = sem("hi_done"), sem("lo_done")
        panels_used = sem("panels_used")
        matmuls_done = sem("matmuls_done")
        act_drained, dve_drained = sem("act_drained"), sem("dve_drained")
        tile_staged, tile_hi, tile_lo = sem("tile_staged"), sem("tile_hi"), sem("tile_lo")
        tables_angle, tables_ready = sem("tables_angle"), sem("tables_ready")
        rope_done, index_summed, mask_ready = sem("rope_done"), sem("index_summed"), sem("mask_ready")
        maxima_ready, exp_done, probs_ready = sem("maxima_ready"), sem("exp_done"), sem("probs_ready")
        pooled = sem("pooled")
        decay_in, decay_exp, decay_log, decay_ready = (
            sem("decay_in"), sem("decay_exp"), sem("decay_log"), sem("decay_ready"))
        variance_ready, deviation_ready, scale_ready = (
            sem("variance_ready"), sem("deviation_ready"), sem("scale_ready"))
        block0_normal, block1_next_normal = sem("block0_normal"), sem("block1_next_normal")
        block1_head_normal, block1_tail_normal = sem("block1_head_normal"), sem("block1_tail_normal")
        final_by_dve, final_by_pool = sem("final_by_dve"), sem("final_by_pool")
        affine_done, zeroed, eps_set = sem("affine_done"), sem("zeroed"), sem("eps_set")
        dve_step, act_step, pool_step = sem("dve_step"), sem("act_step"), sem("pool_step")

        drained = {"act": act_drained, "dve": dve_drained, "staged": tile_staged, "lo": tile_lo}

        def wait_drained(eng, tenant, part=None):
            if tenant.need is not None:
                who, value = tenant.need
                eng.wait_ge(drained[who], value if part is None else part * stride[who] + value)

        def wait_complete(eng, tenant, end, part=None):
            if tenant.full is not None:
                eng.wait_ge(matmuls_done, tenant.full if part is None else part * stride["matmuls"] + tenant.full)
            else:
                eng.wait_ge(panels_used, end if part is None else part * first["stride"] + end)

        def slot(c):
            return c % RAW

        def later(value, laps, per_lap):
            return value if isinstance(laps, int) and laps == 0 else laps * per_lap + value

        order = list(range(HEADS, KT)) + list(range(HEADS))

        block = ctx.enter_context(nc.Block())

        @block.sync
        def _(sp):
            def panel(c, laps, src, shape=None):
                if c >= RAW:
                    sp.wait_ge(lo_done, later(c - RAW + 1, laps, GROUP))
                dst = raw[:, slot(c), :]
                if shape:
                    dst = dst[:, 0:shape[0] * shape[1]].rearrange("p (k n) -> p k n", n=shape[1])
                sp.dma_start(dst, src).then_inc(landed[slot(c)], 16)

            def columns(c0, w, col):
                with sp.Fori(0, KT // GROUP) as g:
                    for j in range(GROUP):
                        panel(c0 + j, g, w[bass.ds(g * (GROUP * P) + j * P, P), col:col + PANEL])

            def rows_in_order(c0, w, col, tiles):
                for j, t in enumerate(tiles):
                    panel(c0 + j, 0, w[t * P:(t + 1) * P, col:col + PANEL])

            def gain_and_offset(i, before, value):
                sp.wait_ge(before, value)
                sp.dma_start(gain, a["ln_g"][i // 3, i % 3:i % 3 + 1, :].to_broadcast([P, D])).then_inc(gain_in, 16)
                sp.dma_start(offset, a["ln_b"][i // 3, i % 3:i % 3 + 1, :].to_broadcast([P, D])).then_inc(gain_in, 16)

            sp.dma_start(cst[:, 0:P], consts[:, 0:P]).then_inc(ident_in, 16)
            w = a["ca_w_kv"][0]
            for j in range(GROUP):
                quarter = slice(j * 512, (j + 1) * 512)
                for b in range(TB):
                    sp.dma_start(mem_tok[:, b, quarter], mem_view[:, b, quarter]).then_inc(mem_arrived[j], 16)
                panel(j, 0, w[j * P:(j + 1) * P, 0:PANEL])
            sp.dma_start(cst[:, P:C_END], consts[:, P:C_END]).then_inc(consts_in, 16)
            sp.dma_start(vec[:, :], vectors).then_inc(vectors_in, 16)
            sp.dma_start(tall[:, 0, :].bitcast(I32), pos.to_broadcast([P, S])).then_inc(positions_in, 16)
            with sp.Fori(1, KT // GROUP) as g:
                for j in range(GROUP):
                    sp.wait_ge(lo_done, g * GROUP + (j - RAW + 1))
                    sp.dma_start(raw[:, slot(j), :], w[bass.ds(g * (GROUP * P) + j * P, P), 0:PANEL]
                                 ).then_inc(landed[slot(j)], 16)
            for b in range(TB):
                sp.dma_start(x[:, b, :], x_view[:, b, :]).then_inc(x_arrived, 16)
            columns(first["kv", 1], a["ca_w_kv"][1], 0)
            for L in range(DEPTH):
                w = w_mix[L]
                if L == 0:
                    columns(first["qi", 0], w, 4 * HALF)
                    kw = w[:, 4 * HALF + HALF:4 * HALF + HALF + IDX_DIM + IDX_HEADS].rearrange(
                        "(k p) n -> p k n", p=P)
                    for j in range(2):
                        panel(first["kw"] + j, 0, kw[:, 8 * j:8 * j + 8, :], (8, IDX_DIM + IDX_HEADS))
                    columns(first["q", L], w, HALF)
                    columns(first["k", L], w, 2 * HALF)
                    columns(first["v", L], w, 3 * HALF)
                    columns(first["u", L], w, 0)
                else:
                    columns(first["q", L], w, 3 * HALF)
                    columns(first["k", L], w, 4 * HALF)
                    panel(first["f"], 0, w[:, 6 * HALF:6 * HALF + HEADS].rearrange("(k p) n -> p k n", p=P),
                          (KT, HEADS))
                    columns(first["v", L], w, 5 * HALF)
                    columns(first["u", L], w, 0)
                    columns(first["gc", L], w, 2 * HALF)
                    columns(first["gb", L], w, HALF)
                rows_in_order(first["out", L, 0], w_out[L], 0, order[0:GROUP])
                if L == 0:
                    sp.wait_ge(matmuls_done, use["z", L][-1].full)
                    sp.dma_start(area_b[:, :, :], pool_w).then_inc(pool_w_in, 16)
                rows_in_order(first["out", L, 0] + GROUP, w_out[L], 0, order[GROUP:])
                gain_and_offset(3 * L, matmuls_done, use["o", L][-1].full)
                rows_in_order(first["out", L, 1], w_out[L], HALF, order)
                wq = a["ca_w_q"][L].rearrange("(k p) n -> p k n", p=P)
                for j in range(KT // 2):
                    panel(first["xq", L] + j, 0, wq[:, 2 * j:2 * j + 2, :], (2, XW))
                for c in range(2):
                    rows_in_order(first["xout", L, c], a["ca_w_o"][L], c * HALF, range(XHEADS))
                gain_and_offset(3 * L + 1, affine_done, 3 * L + 1)

                def part(i, units, base, reg):
                    laps = 0 if reg is None else reg * (first["stride"] // GROUP)
                    for j in range(units):
                        c0 = first["in", L, i, j]
                        with sp.Fori(0, KT // GROUP) as g:
                            for t in range(GROUP):
                                rows = bass.ds(g * (GROUP * P) + t * P, P)
                                if reg is None:
                                    cols = slice((base + j) * FU, (base + j + 1) * FU)
                                else:
                                    cols = bass.ds(reg * (PART_UNITS * FU) + j * FU, FU)
                                src = w_up[L, rows, :, cols]
                                panel(c0 + t, g if reg is None else g + laps, src, (2, FU))
                    for c in range(2):
                        c0 = first["down", L, i, c]
                        with sp.Fori(0, units) as g:
                            for t in range(GROUP):
                                if reg is None:
                                    row = g * (GROUP * P) + (base * FU + t * P)
                                else:
                                    row = g * (GROUP * P) + reg * (PART_UNITS * FU) + t * P
                                src = w_down[L, bass.ds(row, P), c * HALF:(c + 1) * HALF]
                                panel(c0 + t, g if reg is None else g + laps, src)

                with sp.Fori(0, PARTS) as i:
                    part(0, PART_UNITS, 0, i)
                part(PARTS, LAST_UNITS, PARTS * PART_UNITS, None)
                gain_and_offset(3 * L + 2, affine_done, 3 * L + 2)
            for by, n, b, j in ((final_by_dve, 1, 1, 0), (final_by_pool, 1, 0, 0), (final_by_dve, 2, 1, 1),
                                (final_by_dve, 3, 1, 2), (final_by_pool, 2, 0, 1), (final_by_dve, 4, 1, 3),
                                (final_by_pool, 3, 0, 2), (final_by_dve, 5, 0, 3)):
                sp.wait_ge(by, n)
                cols = slice(j * 512, (j + 1) * 512)
                sp.dma_start(out_view[:, b, cols], x[:, b, cols]).then_inc(stored, 16)
            sp.wait_ge(stored, 16 * TB * 4)

        @block.gpsimd
        def _(pool):
            steps = 0

            def step(ins):
                nonlocal steps
                steps += 1
                ins.then_inc(pool_step, 1)
                pool.wait_ge(pool_step, steps)

            def split_low(c, count):
                pool.wait_ge(lo_done, c)
                with pool.Fori(0, count // GROUP) as g:
                    for j in range(GROUP):
                        s = slot(c + j)
                        pool.wait_ge(hi_done, g * GROUP + (c + j + 1))
                        pool.tensor_tensor(w_lo[:, s, :], raw[:, s, :], w_hi[:, s, :].bitcast(F32),
                                           ALU.subtract).then_inc(lo_done, 1)

            pool.memset(area_a[:, :, 0:PAD], 0.0).then_inc(zeroed, 1)
            pool.memset(eps, EPS).then_inc(eps_set, 1)

            pool.wait_ge(positions_in, 16)
            pool.wait_ge(consts_in, 16)
            pos_f = tall[:, 1, :]
            step(pool.tensor_copy(pos_f, tall[:, 0, :].bitcast(I32)))
            magic = 1.5 * 2.0 ** 23
            for t, freq in ((0, C_FREQ_Q), (1, C_FREQ_I)):
                ang, n, m, tmp = tables[:, 2 * t + 1, :], tall[:, 2, :], tall[:, 3, :], tall[:, 0, :]
                step(pool.tensor_scalar(ang, pos_f, cst[:, freq:freq + 1], None, ALU.mult))
                step(pool.tensor_scalar(n, ang, 1.0 / TWO_PI, magic, ALU.mult, ALU.add))
                step(pool.tensor_scalar(n, n, -magic, None, ALU.add))
                step(pool.tensor_scalar(m, n, 1.0 / 4096, magic, ALU.mult, ALU.add))
                step(pool.tensor_scalar(m, m, -magic, 4096.0, ALU.add, ALU.mult))
                step(pool.tensor_tensor(n, n, m, ALU.subtract))
                for part in two_pi_parts():
                    for f in (m, n):
                        step(pool.tensor_scalar(tmp, f, -part, None, ALU.mult))
                        step(pool.tensor_tensor(ang, ang, tmp, ALU.add))
                limit = 3.1415925
                step(pool.tensor_scalar(ang, ang, limit, -limit, ALU.min, ALU.max))
                step(pool.tensor_scalar(tmp, ang, 0.0, 2.0, ALU.max, ALU.mult))
                step(pool.tensor_tensor(tmp, tmp, ang, ALU.subtract))
                pool.tensor_scalar(tables[:, 2 * t, :], tmp, -1.0, TWO_PI / 4,
                                   ALU.mult, ALU.add).then_inc(tables_angle, 1)
                pool.wait_ge(tables_angle, t + 1)

            def normalize_tail(i):
                pool.wait_ge(scale_ready, TB * i + 2)
                part = x[:, 1, HALF:D]
                pool.tensor_scalar(part, part, mv[:, 1, 0:1], rstd[:, 1:2],
                                   ALU.subtract, ALU.mult).then_inc(block1_tail_normal, 1)

            def affine(i, last_transpose):
                normalize_tail(i)
                pool.wait_ge(gain_in, 32 * (i + 1))
                pool.wait_ge(matmuls_done, last_transpose)
                for b in range(TB):
                    step(pool.tensor_tensor(x[:, b, :], x[:, b, :], gain, ALU.mult))
                    ins = pool.tensor_tensor(x[:, b, :], x[:, b, :], offset, ALU.add)
                    if i % 3 == 1:
                        step(ins)
                        ins = pool.tensor_scalar(x[:, b, :], x[:, b, :], ALPHA, None, ALU.mult)
                    if b < TB - 1:
                        step(ins)
                ins.then_inc(affine_done, 1)

            for L in range(DEPTH):
                if L == 0:
                    split_low(first["q", L], 4 * KT + 2 * GROUP)
                else:
                    split_low(first["u", L], 3 * KT)
                affine(3 * L, use["ln_t", L, 0][-1].full)
                affine(3 * L + 1, use["ln_t", L, 1][-1].full)
                if L < DEPTH - 1:
                    affine(3 * L + 2, use["ln_t", L, 2][-1].full)
            pool.wait_ge(gain_in, 32 * 3 * DEPTH)
            for j in range(3):
                if j % 2 == 0:
                    pool.wait_ge(block0_normal, 2 * (3 * DEPTH - 1) + j // 2 + 1)
                cols = slice(j * 512, (j + 1) * 512)
                step(pool.tensor_tensor(x[:, 0, cols], x[:, 0, cols], gain[:, cols], ALU.mult))
                pool.tensor_tensor(x[:, 0, cols], x[:, 0, cols], offset[:, cols], ALU.add).then_inc(final_by_pool, 1)

        @block.scalar
        def _(act):
            def split_high(c, count):
                def one(c, laps):
                    s = slot(c)
                    act.wait_ge(landed[s], later(16 * (c // RAW + 1), laps, 16))
                    if c >= SPLIT:
                        act.wait_ge(panels_used, later(c - SPLIT + 1, laps, GROUP))
                    act.activation(w_hi[:, s, :], raw[:, s, :], ACT.Copy).then_inc(hi_done, 1)
                if count % GROUP == 0 and count > GROUP:
                    with act.Fori(0, count // GROUP) as g:
                        for j in range(GROUP):
                            one(c + j, g)
                else:
                    for j in range(count):
                        one(c + j, 0)

            def high_from_bank(ps, dst):
                act.activation(dst, ps, ACT.Copy).then_inc(tile_hi, 1)

            def high_from_stage(t, r, dst, width):
                act.wait_ge(tile_staged, r + 1)
                act.activation(dst, stage[:, t % 2, 0:width], ACT.Copy).then_inc(tile_hi, 1)

            def tiles2(dst, j):
                return dst[:, 2 * j * S:2 * (j + 1) * S]

            def drain(dst, src, func=ACT.Copy, scale=1.0):
                act.activation(dst, src, func, scale=scale).then_inc(act_drained, 1)

            act.wait_ge(zeroed, 1)
            act.wait_ge(eps_set, 1)
            act.activation(warm[:, 0:1], area_a[:, 0, 0:1], ACT.Copy).then_inc(act_step, 1)
            for g, t in enumerate(use["mem_t"]):
                act.wait_ge(matmuls_done, t.full)
                high_from_bank(psum[:, t.bank, :], tiles2(c_hi, g))
                split_high(first["kv", 0] + (g + 1 if g else 0), 1 if g else 2)
            split_high(first["kv", 0] + KT // 2 + 1, KT // 2 - 1)

            def evacuate_kv(L):
                act.wait_ge(panels_used, first["kv", L] + KT)
                for b, t in enumerate(use["kv", L]):
                    dst = (k_mem[:, L, 2 * b:2 * b + 2, :].rearrange("p h s -> p (h s)") if b < 2
                           else v_mem[:, L, b - 2, :])
                    drain(dst, psum[:, t.bank, :])

            split_high(first["kv", 1], GROUP)
            evacuate_kv(0)
            split_high(first["kv", 1] + GROUP, 7)
            for g, t in enumerate(use["x_t"]):
                act.wait_ge(matmuls_done, t.full)
                high_from_bank(psum[:, t.bank, :], tiles2(x_hi, g))
                split_high(first["kv", 1] + 11 + g, 1)
            evacuate_kv(1)
            split_high(first["qi", 0] + 3, 1)
            act.wait_ge(tables_angle, 2)
            act.activation(tables[:, :, :], tables[:, :, :], ACT.Sin).then_inc(tables_ready, 1)

            def evacuate(name, L, dst):
                end = first[name, L] + KT
                split_high(end, CLOSE)
                for b, t in enumerate(use[name, L]):
                    wait_complete(act, t, end)
                    drain(dst(b), psum[:, t.bank, :])
                split_high(end + CLOSE, GROUP - CLOSE)

            def v_part(b):
                return v_sb[:, b // 2, (b % 2) * 512:(b % 2 + 1) * 512]

            def pair(area):
                return lambda b: area[:, 2 * b:2 * b + 2, :].rearrange("p h s -> p (h s)")

            def u_pair(b):
                return area_a[:, 2 * b:2 * b + 2, PAD:PW]

            def evacuate_u(L):
                act.wait_ge(panels_used, first["u", L] + KT)
                for b, t in enumerate(use["u", L]):
                    drain(u_pair(b), psum[:, t.bank, :].rearrange("p (h s) -> p h s", h=2))

            def head_exp(h):
                act.wait_ge(maxima_ready, maxima0 + h + 1)
                z = probs[:, h % 2, :]
                act.activation(z[:, 0:P], z[:, 0:P], ACT.Exp, bias=neg_max[:, h, 0:1], scale=SCALE,
                               accum_out=sums[:, h, 0:1]).then_inc(exp_done, 1)
                act.activation(z[:, P:P + S], z[:, P:P + S], ACT.Exp, bias=neg_max[:, h, 1:2], scale=SCALE,
                               accum_out=sums[:, h, 1:2]).then_inc(exp_done, 1)

            maxima0 = 0
            for L in range(DEPTH):
                maxima0 = L * (HEADS + XHEADS)
                if L == 0:
                    split_high(first["qi", 0] + GROUP, KT - GROUP)
                    evacuate("qi", L, pair(qi_sb))
                    split_high(first["q", L] + 2, 2)
                    act.wait_ge(panels_used, first["kw"] + 2)
                    ps = psum[:, use["kw"][0].bank, 0:S]
                    act.activation(ki[0:IDX_DIM, :], ps[0:IDX_DIM, :], ACT.Copy).then_inc(act_step, 1)
                    act.activation(ki[IDX_DIM:2 * IDX_DIM, :], ps[0:IDX_DIM, :], ACT.Copy).then_inc(act_step, 1)
                    drain(tall[IDX_DIM:IDX_DIM + IDX_HEADS, 0, :],
                          ps[IDX_DIM:IDX_DIM + IDX_HEADS, :])
                    split_high(first["q", L] + GROUP, KT - GROUP)
                    evacuate("q", L, pair(q_sb))
                    for i, (even, t) in enumerate(use["idx"]):
                        act.wait_ge(matmuls_done, t.full)
                        if i >= 2:
                            act.wait_ge(index_summed, i - 1)
                        width = P * (i % TB + 1)
                        drain(relu[:, i % 2, 0:2 * width].rearrange("p (h n) -> p h n", h=2),
                              psum[:, even.bank:even.bank + 2, 0:width], func=ACT.Relu,
                              scale=IDX_DIM ** -0.5)
                    split_high(first["k", L] + GROUP, KT - GROUP)
                    evacuate("k", L, pair(k_sb))
                    split_high(first["v", L] + GROUP, KT - GROUP)
                    evacuate("v", L, v_part)
                else:
                    split_high(first["q", L] + KT // 2 + 1, KT // 2 - 1)
                    act.wait_ge(affine_done, 3 * L)
                    evacuate("q", L, pair(q_sb))
                    split_high(first["k", L] + GROUP, KT - GROUP)
                    evacuate("k", L, pair(k_sb))
                    act.wait_ge(decay_in, 1)
                    act.activation(dtmp, dtmp, ACT.Exp, scale=-1.0).then_inc(decay_exp, 1)
                    act.wait_ge(decay_exp, 1)
                    act.activation(dtmp, dtmp, ACT.Ln, bias=1.0).then_inc(decay_log, 1)
                    split_high(first["v", L] + GROUP - 1, KT - GROUP + 1)
                    evacuate("v", L, v_part)
                per_head = 2 if L == 0 else 4
                ahead = first["u", L] + GROUP
                for h in range(HEADS + 1):
                    if h > 0:
                        t = use["pt", L][h - 1]
                        act.wait_ge(matmuls_done, t.full)
                        drain(probs_t[:, (h - 1) % 2, 0:3 * P], psum[:, t.bank, 0:3 * P])
                    if h < HEADS:
                        head_exp(h)
                        split_high(ahead, per_head // 2)
                        ahead += per_head // 2
                    elif L == 0:
                        evacuate_u(L)
                    if L == 1 and h == HEADS // 2 - 1:
                        split_high(ahead, per_head // 2)
                        ahead += per_head // 2
                        evacuate_u(L)
                    if h > 0:
                        t = use["o", L][h - 1]
                        act.wait_ge(matmuls_done, t.full)
                        j = HEADS + h - 1
                        high_from_bank(psum[:, t.bank, 0:S], c_hi[:, j * S:(j + 1) * S])
                    if h < HEADS and not (L == 1 and h == HEADS // 2 - 1):
                        split_high(ahead, per_head // 2)
                        ahead += per_head // 2
                if L == 1:
                    split_high(ahead, KT - GROUP)
                    split_high(first["out", L, 0], CLOSE)
                for g in range(4):
                    if L == 0:
                        split_high(first["out", L, 0] + GROUP + 2 * g, 2)
                    high_from_stage(tile["branch", L] + g, staged["branch", L] + g, tiles2(c_hi, g), 2 * S)
                    if L == 1 and g == 1:
                        split_high(first["out", L, 0] + CLOSE, GROUP - CLOSE)
                if L == 1:
                    split_high(first["out", L, 0] + GROUP, 2 * GROUP)
                split_high(first["out", L, 0] + 3 * GROUP, GROUP)
                split_high(first["out", L, 1], KT)

                def normalize(i, block, cols, signal):
                    part = x[:, block, cols]
                    act.wait_ge(scale_ready, TB * i + block + 1)
                    act.activation(part, part, ACT.Identity, bias=mean_shift[:, block:block + 1],
                                   scale=rstd[:, block:block + 1]).then_inc(signal, 1)

                def layer_norm(i, following):
                    if following is not None:
                        split_high(following, GROUP - CLOSE_LAST)
                    act.activation(warm[:, 1:2], cst[:, C_ID:C_ID + 1], ACT.Sqrt).then_inc(act_step, 1)
                    for tb in range(TB):
                        act.wait_ge(variance_ready, TB * i + tb + 1)
                        act.activation(dev[:, tb:tb + 1], mv[:, tb, 1:2], ACT.Sqrt,
                                       bias=eps).then_inc(deviation_ready, 1)
                        if tb == 0:
                            if following is not None:
                                split_high(following + 1, 1)
                            normalize(i, 0, slice(0, HALF), block0_normal)
                    if following is not None:
                        normalize(i, 1, slice(512, HALF), block1_next_normal)

                def norm_tiles(L, i, following, count):
                    for j in range(KT):
                        high_from_stage(tile["ln_t", L, i] + j, staged["ln_t", L, i] + j,
                                        x_hi[:, j * S:(j + 1) * S], S)
                        if j == 1:
                            normalize(3 * L + i, 0, slice(HALF, D), block0_normal)
                        if j % 2 and j >= 3 and 1 + j // 2 < count:
                            split_high(following + 1 + j // 2, 1)

                layer_norm(3 * L, first["xq", L])
                norm_tiles(L, 0, first["xq", L], KT // 2)
                act.activation(warm[:, 1:2], cst[:, C_ID:C_ID + 1], ACT.Exp).then_inc(act_step, 1)
                split_high(first["xout", L, 0], 1)
                for b, t in enumerate(use["xq", L]):
                    wait_complete(act, t, first["xq", L] + KT // 2)
                    drain(area_b[:, 2 * b:2 * b + 2, :].rearrange("p h s -> p (h s)"), psum[:, t.bank, :])
                split_high(first["xout", L, 0] + 1, 1)

                def memory_exp(h):
                    t = use["xz", L][h]
                    act.wait_ge(maxima_ready, maxima0 + HEADS + h + 1)
                    z = xprobs(h)
                    for b in range(TB):
                        ins = act.activation(z[:, b, :], psum[:, t.bank, b * S:(b + 1) * S], ACT.Exp,
                                             bias=neg_max[:, HEADS + h, b:b + 1], scale=SCALE,
                                             accum_out=sums[:, HEADS + h, b:b + 1])
                        ins.then_inc(exp_done if b == 0 else act_drained, 1)

                for h in range(XHEADS - 1):
                    memory_exp(h)
                for h in range(XHEADS):
                    t = use["xpt", L][h]
                    act.wait_ge(matmuls_done, t.full)
                    drain(xprobs_t(h), psum[:, t.bank, :])
                    if h == 0:
                        memory_exp(XHEADS - 1)
                    if h > 0:
                        t = use["xo", L][h - 1]
                        act.wait_ge(matmuls_done, t.full)
                        high_from_bank(psum[:, t.bank, 0:S], c_hi[:, (h - 1) * S:h * S])
                t = use["xo", L][-1]
                act.wait_ge(matmuls_done, t.full)
                high_from_bank(psum[:, t.bank, 0:S], c_hi[:, 3 * S:4 * S])
                split_high(first["xout", L, 0] + 2, XHEADS - 2)
                split_high(first["xout", L, 1], GROUP)
                layer_norm(3 * L + 1, first["in", L, 0, 0])
                norm_tiles(L, 1, first["in", L, 0, 0], KT // 2 + 1)

                def count(value, part, per_part):
                    return value if part is None else part * per_part + value

                def split(c, panels, part):
                    def group(laps, size=GROUP):
                        for j in range(size):
                            s = slot(c + j)
                            act.wait_ge(landed[s], later(16 * ((c + j) // RAW + 1), laps, 16))
                            act.wait_ge(panels_used, later(c + j - SPLIT + 1, laps, GROUP))
                            act.activation(w_hi[:, s, :], raw[:, s, :], ACT.Copy).then_inc(hi_done, 1)

                    laps = 0 if part is None else part * (first["stride"] // GROUP)
                    if panels > GROUP and panels % GROUP == 0:
                        with act.Fori(0, panels // GROUP) as g:
                            group(g if part is None else g + laps)
                    else:
                        group(laps, panels)

                def gate_and_up(i, j, part, begun=GROUP):
                    c0 = first["in", L, i, j]
                    units = PART_UNITS if i < PARTS else LAST_UNITS
                    split(c0 + begun, KT - begun, part)
                    split(first["in", L, i, j + 1] if j + 1 < units else first["down", L, i, 0], GROUP, part)
                    act.wait_ge(panels_used, count(c0 + KT, part, first["stride"]))
                    for b, t in enumerate(use["in", L, i, j][0:2]):
                        drain(gate[:, b, :], psum[:, t.bank, :], func=ACT.Silu)
                    for b in range(2):
                        k = tile["in", L, i, j] + b
                        act.wait_ge(tile_staged, count(staged["in", L, i, j] + b + 1, part, stride["staged"]))
                        act.activation(tiles2(c_hi, 2 * j + b), stage[:, k % 2, :],
                                       ACT.Copy).then_inc(tile_hi, 1)

                def down(i, part):
                    units = PART_UNITS if i < PARTS else LAST_UNITS
                    for c in range(2):
                        c0 = first["down", L, i, c]
                        split(c0 + GROUP, (units - 1) * GROUP, part)
                        if c == 0 or i < PARTS:
                            split(c0 + units * GROUP, GROUP, part)

                gate_and_up(0, 0, None, KT // 2 + 1)
                with act.Fori(0, PARTS) as i:
                    for j in range(1, PART_UNITS):
                        gate_and_up(0, j, i)
                    down(0, i)
                    gate_and_up(0, 0, i + 1)
                for j in range(1, LAST_UNITS):
                    gate_and_up(PARTS, j, None)
                down(PARTS, None)
                if L < DEPTH - 1:
                    layer_norm(3 * L + 2, first["q", L + 1])
                    norm_tiles(L, 2, first["q", L + 1], KT // 2 + 1)
                else:
                    layer_norm(3 * L + 2, None)
                    normalize(3 * L + 2, 0, slice(HALF, D), block0_normal)

        @block.vector
        def _(dve):
            steps = 0

            def step(ins):
                nonlocal steps
                steps += 1
                ins.then_inc(dve_step, 1)
                dve.wait_ge(dve_step, steps)

            def split_group(c, laps):
                for j in range(GROUP):
                    s = slot(c + j)
                    dve.wait_ge(hi_done, later(c + j + 1, laps, GROUP))
                    dve.tensor_tensor(w_lo[:, s, :], raw[:, s, :], w_hi[:, s, :].bitcast(F32),
                                      ALU.subtract).then_inc(lo_done, 1)

            def split_low(c, count):
                if count > GROUP and count % GROUP == 0:
                    with dve.Fori(0, count // GROUP) as g:
                        split_group(c, g)
                elif count == GROUP:
                    split_group(c, 0)
                else:
                    for j in range(count):
                        s = slot(c + j)
                        dve.wait_ge(hi_done, c + j + 1)
                        dve.tensor_tensor(w_lo[:, s, :], raw[:, s, :], w_hi[:, s, :].bitcast(F32),
                                          ALU.subtract).then_inc(lo_done, 1)

            def low(t, dst_hi, dst_lo, src):
                dve.wait_ge(tile_hi, t + 1)
                dve.tensor_tensor(dst_lo, src, dst_hi.bitcast(F32), ALU.subtract).then_inc(tile_lo, 1)

            def tiles2(dst, j):
                return dst[:, 2 * j * S:2 * (j + 1) * S]

            def place_free(t):
                dve.wait_ge(tile_lo, t - 1)

            for g, t in enumerate(use["mem_t"]):
                low(tile["mem_t"] + g, tiles2(c_hi, g), tiles2(c_lo, g), psum[:, t.bank, :])
                split_low(first["kv", 0] + (g + 1 if g else 0), 1 if g else 2)
            split_low(first["kv", 0] + KT // 2 + 1, KT // 2 - 1)
            split_low(first["kv", 1], 11)
            for g, t in enumerate(use["x_t"]):
                low(tile["x_t"] + g, tiles2(x_hi, g), tiles2(x_lo, g), psum[:, t.bank, :])
                split_low(first["kv", 1] + 11 + g, 1)
            split_low(first["qi", 0] + 3, 1)
            dve.wait_ge(tables_ready, 1)
            step(dve.tensor_scalar(tables[:, 1, :], tables[:, 1, :], cst[:, C_SIGN_Q:C_SIGN_Q + 1], None, ALU.mult))
            step(dve.tensor_scalar(tables[:, 3, :], tables[:, 3, :], cst[:, C_SIGN_I:C_SIGN_I + 1], None, ALU.mult))

            def rope(area, rows, t, half):
                heads = area.shape[1]
                mask = list(range(half, 2 * half)) + list(range(half)) + list(range(2 * half, 32))
                tmp = rope_tmp[0:rows, 0:heads * S].rearrange("p (h s) -> p h s", h=heads)
                cos = tables[0:rows, 2 * t:2 * t + 1, :].to_broadcast([rows, heads, S])
                sin = tables[0:rows, 2 * t + 1:2 * t + 2, :].to_broadcast([rows, heads, S])
                step(dve.stream_shuffle(tmp, area, mask))
                step(dve.tensor_tensor(tmp, tmp, sin, ALU.mult))
                step(dve.tensor_tensor(area, area, cos, ALU.mult))
                dve.tensor_tensor(area, area, tmp, ALU.add).then_inc(rope_done, 1)

            def probabilities(h, blocks):
                step(dve.reciprocal(rec[:, h, :], sums[:, h, :]))
                for b in range(TB):
                    ins = dve.tensor_scalar(blocks[b], blocks[b], rec[:, h, b:b + 1], None, ALU.mult)
                    if b == 0:
                        step(ins)
                    else:
                        ins.then_inc(probs_ready, 1)

            def add_to_x(t, b, c, scale):
                tb, chunk = b // 2, 2 * c + b % 2
                part = x[:, tb, chunk * 512:(chunk + 1) * 512]
                dve.scalar_tensor_tensor(out=part, in0=part, scalar=scale, in1=psum[:, t.bank, :],
                                         op0=ALU.mult, op1=ALU.add).then_inc(dve_drained, 1)
                dve.wait_ge(dve_drained, t.drain[1])
                step(dve.bn_stats(stats[:, tb, chunk, :], part))

            def add_first_half(tenants, end, scale):
                split_low(end, CLOSE)
                for b, t in enumerate(tenants):
                    if b == 2:
                        split_low(end + CLOSE, GROUP - CLOSE)
                    wait_complete(dve, t, end)
                    add_to_x(t, b, 0, scale)

            def add_and_normalize(i, tenants, end, following):
                def scale(tb):
                    dve.wait_ge(deviation_ready, TB * i + tb + 1)
                    step(dve.reciprocal(rstd[:, tb:tb + 1], dev[:, tb:tb + 1]))

                def shift(tb):
                    dve.scalar_tensor_tensor(out=mean_shift[:, tb:tb + 1], in0=mv[:, tb, 0:1], scalar=-1.0,
                                             in1=rstd[:, tb:tb + 1], op0=ALU.mult,
                                             op1=ALU.mult).then_inc(scale_ready, 1)

                if following is not None:
                    split_low(following, GROUP - CLOSE_LAST)
                for b, t in enumerate(tenants):
                    wait_complete(dve, t, end)
                    add_to_x(t, b, 1, 1.0 if i % 3 == 2 else ALPHA)
                    if b == 2:
                        scale(0)
                        shift(0)
                    if b % 2:
                        tb = b // 2
                        dve.bn_aggr(mv[:, tb, :], stats[:, tb, :, :].rearrange("p c n -> p (c n)")
                                    ).then_inc(variance_ready, 1)
                scale(1)
                if following is not None:
                    for k in range(2):
                        part = x[:, 1, k * 256:(k + 1) * 256]
                        dve.tensor_scalar(part, part, mv[:, 1, 0:1], rstd[:, 1:2],
                                          ALU.subtract, ALU.mult).then_inc(block1_head_normal, 1)
                shift(1)

            def norm_tiles(L, i, following, count):
                def low_part(j):
                    k = tile["ln_t", L, i] + j
                    low(k, x_hi[:, j * S:(j + 1) * S], x_lo[:, j * S:(j + 1) * S], stage[:, k % 2, 0:S])
                    if j % 2 and 1 + j // 2 < count:
                        split_low(following + 1 + j // 2, 1)

                for j in range(KT):
                    t = use["ln_t", L, i][j // 2]
                    k = tile["ln_t", L, i] + j
                    place_free(k)
                    dve.wait_ge(matmuls_done, t.full)
                    v = (3 * L + i) * KT + j
                    dve.tensor_scalar(stage[:, k % 2, 0:S], psum[:, t.bank, (j % 2) * S:(j % 2 + 1) * S],
                                      vec[:, V_G + v:V_G + v + 1], vec[:, V_B + v:V_B + v + 1],
                                      ALU.mult, ALU.add).then_inc(tile_staged, 1)
                    if j > 0:
                        low_part(j - 1)
                low_part(KT - 1)

            def head_logits(L, h):
                t = use["z", L][h]
                dve.wait_ge(matmuls_done, t.full)
                if h >= 2:
                    dve.wait_ge(matmuls_done, use["pt", L][h - 2].full)
                z, ps = probs[:, h % 2, 0:P + S], psum[:, t.bank, 0:P + S]
                if L == 0:
                    ins = dve.scalar_tensor_tensor(out=z, in0=ps, scalar=1.0, in1=score,
                                                   op0=ALU.mult, op1=ALU.add)
                else:
                    step(dve.scalar_tensor_tensor(out=z[:, 0:P], in0=ps[:, 0:P], scalar=decay_tok[:, 0, h:h + 1],
                                                  in1=causal[:, 0:P], op0=ALU.add, op1=ALU.add))
                    ins = dve.scalar_tensor_tensor(out=z[:, P:P + S], in0=ps[:, P:P + S],
                                                   scalar=decay_tok[:, 1, h:h + 1],
                                                   in1=causal[:, P:P + S], op0=ALU.add, op1=ALU.add)
                ins.then_inc(dve_drained, 1)
                dve.wait_ge(dve_drained, t.drain[1])
                for b in range(TB):
                    step(dve.tensor_reduce(neg_max[:, h, b:b + 1], z[:, 0:P] if b == 0 else z[:, P:P + S], AX, ALU.max))
                dve.tensor_scalar(neg_max[:, h, :], neg_max[:, h, :], -SCALE, None, ALU.mult).then_inc(maxima_ready, 1)

            def head_probs(L, h):
                dve.wait_ge(exp_done, L * (2 * HEADS + XHEADS) + 2 * (h + 1))
                z = probs[:, h % 2, :]
                probabilities(h, (z[:, 0:P], z[:, P:P + S]))

            causal = bias[:, 0, :]

            for L in range(DEPTH):
                if L == 0:
                    split_low(first["qi", L] + GROUP, KT - GROUP)
                    split_low(first["kw"], 2)
                    dve.wait_ge(zeroed, 1)
                    for b, t in enumerate(use["qi", L]):
                        dve.wait_ge(act_drained, t.drain[1])
                        rope(qi_sb[:, 2 * b:2 * b + 2, :], P, 1, 8)
                        dve.wait_ge(rope_done, b + 1)
                    dve.wait_ge(act_drained, use["kw"][0].drain[1])
                    rope(ki[:, :].unsqueeze(1), P, 1, 8)
                    t = use["wi_t"]
                    dve.wait_ge(matmuls_done, t.full)
                    dve.tensor_scalar(wi_tok, psum[:, t.bank, 0:TB * IDX_HEADS].rearrange("p (b h) -> p b h", b=TB),
                                      IDX_HEADS ** -0.5, None, ALU.mult).then_inc(dve_drained, 1)
                    dve.wait_ge(dve_drained, t.drain[1])
                    for i, (_, t) in enumerate(use["idx"]):
                        dve.wait_ge(act_drained, t.drain[1])
                        tb, width = i % TB, P * (i % TB + 1)
                        acc = score[:, 0:P] if tb == 0 else score[:, P:P + S]
                        for j in range(2):
                            h = 2 * (i // TB) + j
                            base = acc if h else cst[:, C_ADMIT + tb * P:C_ADMIT + tb * P + width]
                            ins = dve.scalar_tensor_tensor(
                                out=acc, in0=relu[:, i % 2, j * width:(j + 1) * width],
                                scalar=wi_tok[:, tb, h:h + 1], in1=base, op0=ALU.mult, op1=ALU.add)
                            if j == 0:
                                step(ins)
                            else:
                                ins.then_inc(index_summed, 1)
                                dve.wait_ge(index_summed, i + 1)
                    for b, t in enumerate(use["q", L]):
                        dve.wait_ge(act_drained, t.drain[1])
                        rope(q_sb[0:32, 2 * b:2 * b + 2, :], 32, 0, 16)
                        dve.wait_ge(rope_done, 5 + b + 1)
                    for r in range(TOPK // 8):
                        for tb in range(TB):
                            rows = slice(0, P) if tb == 0 else slice(P, P + S)
                            src = score if r == 0 else work
                            step(dve.max(top8[:, tb, :], src[:, rows]))
                            step(dve.match_replace(work[:, rows], top8[:, tb, :], src[:, rows], TAKEN))
                    dve.tensor_scalar(score, work, (TAKEN + NOT_ADMITTED) / 2, MASKED,
                                      ALU.is_gt, ALU.mult).then_inc(mask_ready, 1)
                    for b, t in enumerate(use["k", L]):
                        dve.wait_ge(act_drained, t.drain[1])
                        rope(k_sb[0:32, 2 * b:2 * b + 2, :], 32, 0, 16)
                        dve.wait_ge(rope_done, 9 + b + 1)
                    dve.wait_ge(mask_ready, 1)
                else:
                    split_low(first["q", L] + KT // 2 + 1, KT // 2 - 1)
                    split_low(first["k", L], KT)
                    split_low(first["f"], 1)
                    split_low(first["v", L], GROUP - 1)
                    step(dve.memset(causal[:, P:S], 0.0))
                    step(dve.tensor_copy(causal[:, 0:P], cst[:, C_TRI:C_TRI + P]))
                    step(dve.tensor_copy(causal[:, S:P + S], cst[:, C_TRI:C_TRI + P]))
                    step(dve.memset(ones8, 1.0))
                    t = use["f"][0]
                    dve.wait_ge(panels_used, first["f"] + 1)
                    ps = psum[0:HEADS, t.bank, 0:S]
                    dve.tensor_scalar(decay, ps, vec[0:HEADS, V_FB:V_FB + 1], None, ALU.add).then_inc(dve_drained, 1)
                    dve.wait_ge(dve_drained, t.drain[1])
                    step(dve.tensor_scalar(dtmp, decay, 0.0, 2.0, ALU.max, ALU.mult))
                    dve.tensor_tensor(dtmp, dtmp, decay, ALU.subtract).then_inc(decay_in, 1)
                    dve.wait_ge(decay_in, 1)
                    step(dve.tensor_scalar(decay, decay, 0.0, None, ALU.min))
                    dve.wait_ge(decay_log, 1)
                    step(dve.tensor_tensor(decay, decay, dtmp, ALU.subtract))
                    step(dve.tensor_scalar(neg_decay, decay, -1.0 / SCALE, None, ALU.mult))
                    step(dve.tensor_tensor_scan(dtmp, ones8, neg_decay, 0.0, ALU.mult, ALU.add))
                    step(dve.tensor_copy(neg_decay, dtmp))
                    dve.tensor_scalar(decay, dtmp, -1.0, None, ALU.mult).then_inc(decay_ready, 1)
                    split_low(first["v", L] + GROUP - 1, KT - GROUP + 1)
                    t = use["ft"]
                    dve.wait_ge(matmuls_done, t.full)
                    dve.tensor_copy(decay_tok, psum[:, t.bank, 0:TB * HEADS].rearrange(
                        "p (b h) -> p b h", b=TB)).then_inc(dve_drained, 1)
                    dve.wait_ge(dve_drained, t.drain[1])

                for h in range(HEADS + 1):
                    if h < HEADS:
                        head_logits(L, h)
                        head_probs(L, h)
                    if h > 0:
                        t = use["o", L][h - 1]
                        j = HEADS + h - 1
                        low(tile["o", L] + h - 1, c_hi[:, j * S:(j + 1) * S], c_lo[:, j * S:(j + 1) * S],
                            psum[:, t.bank, 0:S])
                    if L == 1 and h == HEADS - 1:
                        dve.wait_ge(panels_used, first["gc", L] + KT)
                        for b, t in enumerate(use["gc", L]):
                            dve.wait_ge(act_drained, use["u", L][b].drain[1])
                            u = area_a[:, 2 * b:2 * b + 2, PAD:PW]
                            dve.tensor_tensor(u, psum[:, t.bank, :].rearrange("p (h s) -> p h s", h=2), u,
                                              ALU.mult).then_inc(dve_drained, 1)
                split_from = first["out", L, 0]
                if L == 0:
                    for z in (ping, pong):
                        step(dve.memset(z[:, :, 0:PAD], 0.0))
                    dve.wait_ge(act_drained, use["u", L][-1].drain[1])
                    def pool_group(g):
                        window = WINDOWS[g]
                        u = area_a[:, 2 * g:2 * g + 2, :]
                        src, dst, shift = u, ping, 1
                        while shift < window:
                            step(dve.tensor_tensor(dst[:, :, PAD:PW], src[:, :, PAD:PW],
                                                   src[:, :, PAD - shift:PW - shift], ALU.add))
                            src, dst, shift = dst, (pong if dst is ping else ping), 2 * shift
                        inv = cst[:, C_INVC + g * PAD:C_INVC + g * PAD + window].unsqueeze(1).to_broadcast(
                            [P, 2, window])
                        step(dve.tensor_tensor(src[:, :, PAD:PAD + window], src[:, :, PAD:PAD + window], inv, ALU.mult))
                        dve.scalar_tensor_tensor(out=u[:, :, PAD:PW], in0=src[:, :, PAD:PW],
                                                 scalar=1.0 / window, in1=u[:, :, PAD:PW],
                                                 op0=ALU.mult, op1=ALU.subtract).then_inc(pooled, 1)
                        dve.wait_ge(pooled, g + 1)

                    def scale_group(g):
                        k, t = tile["branch", L] + g, use["pool"][g]
                        place_free(k)
                        dve.wait_ge(matmuls_done, t.full)
                        for j in range(2):
                            v = V_SCALE + 2 * g + j
                            ins = dve.tensor_scalar(stage[:, k % 2, j * S:(j + 1) * S],
                                                    psum[:, t.bank, j * S:(j + 1) * S],
                                                    vec[:, v:v + 1], None, ALU.mult)
                            if j == 0:
                                step(ins)
                            else:
                                ins.then_inc(tile_staged, 1)

                    def low_group(g):
                        k = tile["branch", L] + g
                        low(k, tiles2(c_hi, g), tiles2(c_lo, g), stage[:, k % 2, :])

                    pool_group(0)
                    pool_group(1)
                    scale_group(0)
                    pool_group(2)
                    low_group(0)
                    scale_group(1)
                    pool_group(3)
                    low_group(1)
                    dve.wait_ge(lo_done, split_from + 2 * GROUP)
                    split_low(split_from + 2 * GROUP, 2)
                    scale_group(2)
                    low_group(2)
                    split_low(split_from + 2 * GROUP + 2, 2)
                    scale_group(3)
                    low_group(3)
                else:
                    dve.wait_ge(dve_drained, use["gc", L][-1].drain[1])
                    for j in range(HALF // P):
                        w = [vec[:, V_CONV + 3 * j + i:V_CONV + 3 * j + i + 1] for i in range(3)]
                        y = area_b[:, j, :]
                        step(dve.tensor_scalar(y, area_a[:, j, PAD:PW], w[2], None, ALU.mult))
                        for i in (1, 0):
                            step(dve.scalar_tensor_tensor(out=y, in0=area_a[:, j, PAD - 2 + i:PW - 2 + i],
                                                          scalar=w[i], in1=y, op0=ALU.mult, op1=ALU.add))
                    dve.wait_ge(lo_done, split_from)
                    split_low(split_from, CLOSE)
                    for b, t in enumerate(use["gb", L]):
                        if b == 2:
                            split_low(split_from + CLOSE, GROUP - CLOSE)
                        k = tile["branch", L] + b
                        place_free(k)
                        wait_complete(dve, t, first["gb", L] + KT)
                        dve.tensor_tensor(stage[:, k % 2, :], psum[:, t.bank, :],
                                          area_b[:, 2 * b:2 * b + 2, :].rearrange("p h s -> p (h s)"),
                                          ALU.mult).then_inc(tile_staged, 1)
                        low(k, tiles2(c_hi, b), tiles2(c_lo, b), stage[:, k % 2, :])
                    split_low(split_from + GROUP, 2 * GROUP)
                split_low(split_from + 3 * GROUP, GROUP)
                if L > 0:
                    dve.wait_ge(affine_done, 3 * L)
                add_first_half(use["out", L, 0], first["out", L, 0] + KT, ALPHA)
                split_low(first["out", L, 1] + GROUP, KT - GROUP)
                add_and_normalize(3 * L, use["out", L, 1], first["out", L, 1] + KT, first["xq", L])
                norm_tiles(L, 0, first["xq", L], KT // 2)
                split_low(first["xout", L, 0], 1)

                def memory_maxima(h):
                    t = use["xz", L][h]
                    dve.wait_ge(matmuls_done, t.full)
                    step(dve.tensor_reduce(neg_max[:, HEADS + h, :], psum[:, t.bank, :].rearrange(
                        "p (b n) -> p b n", b=TB), AX, ALU.max))
                    dve.tensor_scalar(neg_max[:, HEADS + h, :], neg_max[:, HEADS + h, :], -SCALE, None,
                                      ALU.mult).then_inc(maxima_ready, 1)

                def memory_probs(h):
                    t = use["xz", L][h]
                    dve.wait_ge(exp_done, L * (2 * HEADS + XHEADS) + 2 * HEADS + h + 1)
                    dve.wait_ge(act_drained, t.drain[1])
                    z = xprobs(h)
                    probabilities(HEADS + h, (z[:, 0, :], z[:, 1, :]))

                for h in range(XHEADS + 1):
                    if h < XHEADS:
                        memory_maxima(h)
                    if h > 0:
                        memory_probs(h - 1)
                split_low(first["xout", L, 0] + 1, 1)
                for h, t in enumerate(use["xo", L]):
                    low(tile["xo", L] + h, c_hi[:, h * S:(h + 1) * S], c_lo[:, h * S:(h + 1) * S],
                        psum[:, t.bank, 0:S])
                split_low(first["xout", L, 0] + 2, XHEADS - 2)
                dve.wait_ge(affine_done, 3 * L + 1)
                add_first_half(use["xout", L, 0], first["xout", L, 0] + XHEADS, ALPHA)
                add_and_normalize(3 * L + 1, use["xout", L, 1], first["xout", L, 1] + XHEADS, first["in", L, 0, 0])
                norm_tiles(L, 1, first["in", L, 0, 0], KT // 2 + 1)

                def count(value, part, per_part):
                    return value if part is None else part * per_part + value

                def split(c, panels, part):
                    def group(laps, size=GROUP):
                        for j in range(size):
                            s = slot(c + j)
                            dve.wait_ge(hi_done, later(c + j + 1, laps, GROUP))
                            dve.tensor_tensor(w_lo[:, s, :], raw[:, s, :], w_hi[:, s, :].bitcast(F32),
                                              ALU.subtract).then_inc(lo_done, 1)

                    laps = 0 if part is None else part * (first["stride"] // GROUP)
                    if panels > GROUP and panels % GROUP == 0:
                        with dve.Fori(0, panels // GROUP) as g:
                            group(g if part is None else g + laps)
                    else:
                        group(laps, panels)

                def gate_and_up(i, j, part, begun=GROUP):
                    c0 = first["in", L, i, j]
                    units = PART_UNITS if i < PARTS else LAST_UNITS
                    split(c0 + begun, KT - begun, part)
                    split(first["in", L, i, j + 1] if j + 1 < units else first["down", L, i, 0], GROUP, part)
                    tenants = use["in", L, i, j]
                    dve.wait_ge(panels_used, count(c0 + KT, part, first["stride"]))
                    for b in range(2):
                        k = tile["in", L, i, j] + b
                        dve.wait_ge(tile_lo, count(k - 1, part, stride["lo"]))
                        dve.wait_ge(act_drained, count(tenants[b].drain[1], part, stride["act"]))
                        dve.tensor_tensor(stage[:, k % 2, :], psum[:, tenants[2 + b].bank, :], gate[:, b, :],
                                          ALU.mult).then_inc(tile_staged, 1)
                    for b in range(2):
                        k = tile["in", L, i, j] + b
                        dst = 2 * j + b
                        dve.wait_ge(tile_hi, count(k + 1, part, stride["lo"]))
                        dve.tensor_tensor(tiles2(c_lo, dst), stage[:, k % 2, :],
                                          tiles2(c_hi, dst).bitcast(F32), ALU.subtract).then_inc(tile_lo, 1)

                def down(part):
                    for c in range(2):
                        c0, end = first["down", L, 0, c], first["down", L, 0, c] + PART_UNITS * GROUP
                        split(c0 + GROUP, (PART_UNITS - 1) * GROUP, part)
                        split(end, CLOSE, part)
                        if c == 0:
                            dve.wait_ge(affine_done, 3 * L + 2)
                        for b, t in enumerate(use["down", L, 0, c]):
                            wait_complete(dve, t, end, part)
                            tb, chunk = b // 2, 2 * c + b % 2
                            dst = x[:, tb, chunk * 512:(chunk + 1) * 512]
                            dve.tensor_tensor(dst, psum[:, t.bank, :], dst, ALU.add).then_inc(dve_drained, 1)
                        split(end + CLOSE, GROUP - CLOSE, part)

                gate_and_up(0, 0, None, KT // 2 + 1)
                with dve.Fori(0, PARTS) as i:
                    for j in range(1, PART_UNITS):
                        gate_and_up(0, j, i)
                    down(i)
                    gate_and_up(0, 0, i + 1)
                for j in range(1, LAST_UNITS):
                    gate_and_up(PARTS, j, None)
                c0 = first["down", L, PARTS, 0]
                split_low(c0 + GROUP, (LAST_UNITS - 1) * GROUP)
                add_first_half(use["down", L, PARTS, 0], c0 + LAST_UNITS * GROUP, 1.0)
                c0 = first["down", L, PARTS, 1]
                split_low(c0 + GROUP, (LAST_UNITS - 1) * GROUP)
                following = first["q", L + 1] if L < DEPTH - 1 else None
                add_and_normalize(3 * L + 2, use["down", L, PARTS, 1], c0 + LAST_UNITS * GROUP, following)
                if L < DEPTH - 1:
                    norm_tiles(L, 2, following, KT // 2 + 1)
            dve.wait_ge(gain_in, 32 * 3 * DEPTH)
            for b, j in ((1, 0), (1, 1), (1, 2), (1, 3), (0, 3)):
                part, cols = x[:, b, j * 512:(j + 1) * 512], slice(j * 512, (j + 1) * 512)
                if b == 0:
                    dve.wait_ge(block0_normal, 2 * 3 * DEPTH)
                    step(dve.tensor_tensor(part, part, gain[:, cols], ALU.mult))
                    ins = dve.tensor_tensor(part, part, offset[:, cols], ALU.add)
                else:
                    step(dve.scalar_tensor_tensor(out=part, in0=part, scalar=mv[:, 1, 0:1], in1=gain[:, cols],
                                                  op0=ALU.subtract, op1=ALU.mult))
                    ins = dve.scalar_tensor_tensor(out=part, in0=part, scalar=rstd[:, 1:2], in1=offset[:, cols],
                                                   op0=ALU.mult, op1=ALU.add)
                ins.then_inc(final_by_dve, 1)

        @block.tensor
        def _(pe):
            def passes(pairs, out, start, stop=False):
                (lh, ll), (rh, rl) = pairs
                pe.matmul(out, lh, rh, start=start, stop=False, skip_group_check=True)
                pe.matmul(out, lh, rl, start=False, stop=False, skip_group_check=True)
                return pe.matmul(out, ll, rh, start=False, stop=stop, skip_group_check=True)

            def weight(s, lo_col, width):
                return w_hi[:, s, lo_col:lo_col + width], w_lo[:, s, lo_col:lo_col + width]

            def activations(kind, t, lo_col=0, width=S):
                hi, lo = (x_hi, x_lo) if kind == "x" else (c_hi, c_lo)
                if isinstance(t, int):
                    return hi[:, t * S + lo_col:t * S + lo_col + width], lo[:, t * S + lo_col:t * S + lo_col + width]
                return hi[:, bass.ds(t * S + lo_col, width)], lo[:, bass.ds(t * S + lo_col, width)]

            def panel_split(c, laps=0):
                pe.wait_ge(lo_done, later(c + 1, laps, GROUP))

            def feature_bank(c, tenant, b, t, opening, cols=0, kind="x"):
                for j in range(2):
                    ins = passes((weight(slot(c), cols + (2 * b + j) * P, P), activations(kind, t)),
                                 psum[:, tenant.bank, j * S:(j + 1) * S], opening and j == 0)
                return ins

            def feature_major(c, tenants, kind, t, opening, cols=0, reg=None, last=True):
                for b, tenant in enumerate(tenants):
                    if opening:
                        wait_drained(pe, tenant, reg)
                    ins = feature_bank(c, tenant, b, t, opening, cols, kind)
                if last:
                    ins.then_inc(panels_used, 1)

            def token_bank(c, tenant, b, t, opening, cols=0, chunks=2, kind="c"):
                xh, xl = activations(kind, t, (b // chunks) * P, P)
                wh, wl = weight(slot(c), cols + (b % chunks) * 512, 512)
                out = psum[:, tenant.bank, :]
                pe.matmul(out, xh, wh, start=opening, stop=False, skip_group_check=True)
                pe.matmul(out, xh, wl, start=False, stop=False, skip_group_check=True)
                return pe.matmul(out, xl, wh, start=False, stop=False, skip_group_check=True)

            def token_major(c, tenants, kind, t, opening, cols=0, chunks=2, reg=None):
                for b, tenant in enumerate(tenants):
                    if opening:
                        wait_drained(pe, tenant, reg)
                    ins = token_bank(c, tenant, b, t, opening, cols, chunks, kind)
                ins.then_inc(panels_used, 1)

            def close(c, laps, tenants, count, share):
                for i in range(count):
                    panel_split(c + i, laps)
                for b, tenant in enumerate(tenants):
                    for i in range(count):
                        ins = share(i, b, tenant)
                        if tenant.full is None:
                            ins.then_inc(panels_used, 1)
                    if tenant.full is not None:
                        ins.then_inc(matmuls_done, 1)

            def close_feature_major(c, tenants, tiles):
                close(c, 0, tenants, len(tiles),
                      lambda i, b, tenant: feature_bank(c + i, tenant, b, tiles[i], False))

            def close_token_major(c, laps, tenants, tiles, kind):
                close(c, laps, tenants, len(tiles),
                      lambda i, b, tenant: token_bank(c + i, tenant, b, tiles[i], False, kind=kind))

            def unit(name):
                c0 = first[name]
                for j in range(GROUP):
                    panel_split(c0 + j)
                    feature_major(c0 + j, use[name], "x", j, j == 0)
                with pe.Fori(1, KT // GROUP - 1) as g:
                    for j in range(GROUP):
                        panel_split(c0 + j, g)
                        feature_major(c0 + j, use[name], "x", g * GROUP + j, False)
                for j in range(KT - GROUP, KT - CLOSE):
                    panel_split(c0 + j)
                    feature_major(c0 + j, use[name], "x", j, False)
                close_feature_major(c0 + KT - CLOSE, use[name], range(KT - CLOSE, KT))

            def unit_token_major(name):
                c0 = first[name]
                for j in range(KT - CLOSE):
                    panel_split(c0 + j)
                    token_major(c0 + j, use[name], "x", j, j == 0)
                close_token_major(c0 + KT - CLOSE, 0, use[name], range(KT - CLOSE, KT), "x")

            def transposes(tenant, g, src):
                wait_drained(pe, tenant)
                for j in range(2):
                    for b in range(TB):
                        col = j * S + b * P
                        t = 2 * g + j
                        ins = pe.matmul(psum[:, tenant.bank, col:col + P], src[:, b, t * P:(t + 1) * P], ident,
                                        start=(j == 0 and b == 0), stop=True, is_transpose=True,
                                        skip_group_check=True)
                ins.then_inc(matmuls_done, 1)

            def wait_normal(i, g):
                pe.wait_ge(block0_normal, 2 * i + (1 if g < 4 else 2))
                if g < 2:
                    pe.wait_ge(block1_head_normal, 2 * i + g + 1)
                elif g < 4:
                    pe.wait_ge(block1_next_normal, i + 1)
                else:
                    pe.wait_ge(block1_tail_normal, i + 1)

            def transposed_unit(name, panel, src, tiles_per_batch=1, per_panel=1, count=KT, arrived=None,
                                closing=None, closes=CLOSE):
                def one(g):
                    arrived(g)
                    transposes(use[name][g], g, src)

                for g in range(2):
                    one(g)
                for j in range(count):
                    if closing and j == count - closes:
                        pe.wait_ge(tile_lo, tile[name] + KT // tiles_per_batch)
                        closing()
                        break
                    if per_panel == 1:
                        pe.wait_ge(tile_lo, tile[name] + j // tiles_per_batch + 1)
                    panel(j)
                    if j == 0:
                        one(2)
                    if j + 3 < KT // 2:
                        one(j + 3)

            def kv_panel(L, j):
                c = first["kv", L] + j
                panel_split(c)
                tenants = use["kv", L]
                feature_major(c, tenants[0:2], "c", j, j == 0, last=False)
                token_major(c, tenants[2:4], "c", j, j == 0, XW, 1)

            pe.wait_ge(ident_in, 16)
            transposed_unit("mem_t", lambda j: kv_panel(0, j), mem_tok, tiles_per_batch=2,
                            arrived=lambda g: pe.wait_ge(mem_arrived[g // 2], 16 * TB))
            for j in range(KT):
                kv_panel(1, j)
                if j >= 7 and j < 15:
                    if j == 7:
                        pe.wait_ge(x_arrived, 16 * TB)
                    transposes(use["x_t"][j - 7], j - 7, x)

            def unit_panel(key):
                def run(j):
                    panel_split(first[key] + j)
                    feature_major(first[key] + j, use[key], "x", j, j == 0)
                return run

            def scores(L, h, t):
                wait_drained(pe, t)
                ps = psum[:, t.bank, :]
                for b, cols in ((0, (0, P)), (1, (P, P + S))):
                    width = cols[1] - cols[0]
                    ins = pe.matmul(ps[:, cols[0]:cols[1]], q_sb[:, h, b * P:(b + 1) * P], k_sb[:, h, 0:width],
                                    start=(b == 0), stop=(L == 0), skip_group_check=True)
                    if L == 1:
                        ins = pe.matmul(ps[:, cols[0]:cols[1]],
                                        ident[0:HEADS, h:h + 1].to_broadcast([HEADS, P]),
                                        neg_decay[:, 0:width], start=False, stop=True, skip_group_check=True)
                ins.then_inc(matmuls_done, 1)

            def transpose_probs(L, h, t):
                pe.wait_ge(probs_ready, L * (HEADS + XHEADS) + h + 1)
                wait_drained(pe, t)
                for j in range(3):
                    ins = pe.matmul(psum[:, t.bank, j * P:(j + 1) * P], probs[:, h % 2, j * P:(j + 1) * P], ident,
                                    start=(j == 0), stop=True, is_transpose=True, skip_group_check=True)
                ins.then_inc(matmuls_done, 1)

            def weighted_values(L, h, t):
                pe.wait_ge(act_drained, use["pt", L][h].drain[1])
                wait_drained(pe, t)
                pt = probs_t[:, h % 2, :]
                pe.matmul(psum[:, t.bank, 0:S], v_sb[:, 0, h * HD:(h + 1) * HD], pt[:, 0:S],
                          start=True, stop=False, skip_group_check=True)
                pe.matmul(psum[:, t.bank, P:S], v_sb[:, 1, h * HD:(h + 1) * HD], pt[:, S:S + P],
                          start=False, stop=True, skip_group_check=True).then_inc(matmuls_done, 1)

            for L in range(DEPTH):
                if L == 0:
                    pe.wait_ge(tile_lo, tile["x_t"] + KT // 2)
                    unit(("qi", L))
                    t = use["kw"][0]
                    wide = IDX_DIM + IDX_HEADS
                    for j in range(KT):
                        c = first["kw"] + j // 8
                        if j % 8 == 0:
                            panel_split(c)
                        if j == 0:
                            wait_drained(pe, t)
                        ins = passes((weight(slot(c), (j % 8) * wide, wide), activations("x", j)),
                                     psum[0:wide, t.bank, 0:S], j == 0)
                        if j % 8 == 7:
                            ins.then_inc(panels_used, 1)
                    unit(("q", L))
                    t = use["wi_t"]
                    pe.wait_ge(act_drained, use["kw"][0].drain[1])
                    wait_drained(pe, t)
                    rows = slice(IDX_DIM, IDX_DIM + IDX_HEADS)
                    for b in range(TB):
                        ins = pe.matmul(psum[:, t.bank, b * IDX_HEADS:(b + 1) * IDX_HEADS],
                                        tall[rows, 0, b * P:(b + 1) * P], ident[rows, rows],
                                        start=(b == 0), stop=True, is_transpose=True, skip_group_check=True)
                    ins.then_inc(matmuls_done, 1)
                    pe.wait_ge(rope_done, 5)
                    for i, pair in enumerate(use["idx"]):
                        tb = i % TB
                        width = P * (tb + 1)
                        for j in range(2):
                            rows = slice(j * IDX_DIM, (j + 1) * IDX_DIM)
                            wait_drained(pe, pair[j])
                            ins = pe.matmul(psum[:, pair[j].bank, 0:width],
                                            qi_sb[rows, i // TB, tb * P:(tb + 1) * P], ki[rows, 0:width],
                                            start=True, stop=True)
                        ins.then_inc(matmuls_done, 1)
                    unit(("k", L))
                    unit_token_major(("v", L))
                    pe.wait_ge(rope_done, 13)
                else:
                    transposed_unit(("ln_t", L - 1, 2), unit_panel(("q", L)), x,
                                    arrived=lambda g: wait_normal(3 * L - 1, g),
                                    closing=lambda: close_feature_major(first["q", L] + KT - CLOSE, use["q", L],
                                                                        range(KT - CLOSE, KT)))
                    unit(("k", L))
                    t = use["f"][0]
                    panel_split(first["f"])
                    wait_drained(pe, t)
                    for j in range(KT):
                        ins = passes((weight(slot(first["f"]), j * HEADS, HEADS), activations("x", j)),
                                     psum[0:HEADS, t.bank, 0:S], j == 0)
                    ins.then_inc(panels_used, 1)
                    unit_token_major(("v", L))
                    t = use["ft"]
                    wait_drained(pe, t)
                    pe.wait_ge(decay_ready, 1)
                    for b in range(TB):
                        ins = pe.matmul(psum[:, t.bank, b * HEADS:(b + 1) * HEADS], decay[:, b * P:(b + 1) * P],
                                        ident[0:HEADS, 0:HEADS], start=(b == 0), stop=True, is_transpose=True,
                                        skip_group_check=True)
                    ins.then_inc(matmuls_done, 1)
                    pe.wait_ge(act_drained, use["k", L][-1].drain[1])
                fills = [unit_panel(("u", L))] * KT + ([unit_panel(("gc", L))] * KT if L else [])
                fills = [(f, j % KT) for j, f in enumerate(fills)]
                per_head = len(fills) // HEADS
                for h in range(HEADS + 1):
                    if h < HEADS:
                        scores(L, h, use["z", L][h])
                    if h > 0:
                        transpose_probs(L, h - 1, use["pt", L][h - 1])
                    for i in range(per_head if h < HEADS else 0):
                        if i == per_head // 2 and h > 0:
                            if h == 1:
                                pe.wait_ge(act_drained, use["v", L][-1].drain[1])
                            weighted_values(L, h - 1, use["o", L][h - 1])
                        run, j = fills[h * per_head + i]
                        run(j)
                weighted_values(L, HEADS - 1, use["o", L][HEADS - 1])
                if L == 1:
                    unit(("gb", L))
                def mixed_group(g):
                    tenant = use["pool"][g]
                    wait_drained(pe, tenant)
                    pe.wait_ge(pool_w_in, 16)
                    pe.wait_ge(pooled, g + 1)
                    for d in range(2):
                        for i in range(2):
                            ins = pe.matmul(psum[:, tenant.bank, d * S:(d + 1) * S],
                                            pool_w_sb[:, g, i, d * P:(d + 1) * P],
                                            area_a[:, 2 * g + i, PAD:PW], start=(d == 0 and i == 0), stop=(i == 1),
                                            skip_group_check=True)
                    ins.then_inc(matmuls_done, 1)

                for c in range(2):
                    key = ("out", L, c)
                    for j, t in enumerate(order):
                        if c == 0 and j < HEADS:
                            pe.wait_ge(tile_lo, tile["o", L] + j + 1)
                        if c == 0 and L == 0 and j in (2, 4, 6, 8):
                            mixed_group(j // 2 - 1)
                        if c == 0 and j >= HEADS:
                            pe.wait_ge(tile_lo, tile["branch", L] + (j - HEADS) // 2 + 1)
                        if j < KT - (CLOSE, CLOSE_LAST)[c]:
                            panel_split(first[key] + j)
                            token_major(first[key] + j, use[key], "c", t, j == 0)
                    begin = KT - (CLOSE, CLOSE_LAST)[c]
                    close_token_major(first[key] + begin, 0, use[key], order[begin:], "c")

                def xq_panel(j):
                    c = first["xq", L] + j
                    panel_split(c)
                    for i in range(2):
                        pe.wait_ge(tile_lo, tile["ln_t", L, 0] + 2 * j + i + 1)
                        feature_major(c, use["xq", L], "x", 2 * j + i, j == 0 and i == 0, i * XW, last=(i == 1))

                def xq_closing():
                    c = first["xq", L] + KT // 2 - 1

                    def share(_, b, tenant):
                        for k in range(2):
                            ins = feature_bank(c, tenant, b, KT - 2 + k, False, k * XW)
                        return ins
                    close(c, 0, use["xq", L], 1, share)

                transposed_unit(("ln_t", L, 0), xq_panel, x, per_panel=2, count=KT // 2,
                                arrived=lambda g: wait_normal(3 * L, g), closing=xq_closing, closes=1)
                for h, t in enumerate(use["xz", L]):
                    if h % 2 == 0:
                        pe.wait_ge(act_drained, use["xq", L][h // 2].drain[1])
                    wait_drained(pe, t)
                    for b in range(TB):
                        ins = pe.matmul(psum[:, t.bank, b * S:(b + 1) * S], q_sb[:, h, b * P:(b + 1) * P],
                                        k_mem[:, L, h, :], start=(b == 0), stop=True, skip_group_check=True)
                    ins.then_inc(matmuls_done, 1)
                for h in range(XHEADS + 1):
                    if h < XHEADS:
                        t = use["xpt", L][h]
                        pe.wait_ge(probs_ready, L * (HEADS + XHEADS) + HEADS + h + 1)
                        wait_drained(pe, t)
                        for m in range(2):
                            for b in range(TB):
                                col = m * S + b * P
                                ins = pe.matmul(psum[:, t.bank, col:col + P], xprobs(h)[:, b, m * P:(m + 1) * P],
                                                ident, start=(m == 0 and b == 0), stop=True, is_transpose=True,
                                                skip_group_check=True)
                        ins.then_inc(matmuls_done, 1)
                    if h > 0:
                        t = use["xo", L][h - 1]
                        pe.wait_ge(act_drained, use["xpt", L][h - 1].drain[1])
                        wait_drained(pe, t)
                        for m in range(2):
                            ins = pe.matmul(psum[:, t.bank, 0:S], v_mem[:, L, m, (h - 1) * HD:h * HD],
                                            xprobs_t(h - 1)[:, m * S:(m + 1) * S],
                                            start=(m == 0), stop=(m == 1), skip_group_check=True)
                        ins.then_inc(matmuls_done, 1)
                for c in range(2):
                    key = ("xout", L, c)
                    for j in range(XHEADS):
                        if c == 0:
                            pe.wait_ge(tile_lo, tile["xo", L] + j + 1)
                        if j < XHEADS - (CLOSE, CLOSE_LAST)[c]:
                            panel_split(first[key] + j)
                            token_major(first[key] + j, use[key], "c", j, j == 0)
                    begin = XHEADS - (CLOSE, CLOSE_LAST)[c]
                    close_token_major(first[key] + begin, 0, use[key], range(begin, XHEADS), "c")

                def gate_and_up(i, j, part):
                    laps = 0 if part is None else part * (first["stride"] // GROUP)
                    c0 = first["in", L, i, j]
                    for t in range(GROUP):
                        panel_split(c0 + t, laps)
                        feature_major(c0 + t, use["in", L, i, j], "x", t, t == 0, reg=part)
                    with pe.Fori(1, KT // GROUP) as g:
                        for t in range(GROUP):
                            panel_split(c0 + t, g if part is None else g + laps)
                            feature_major(c0 + t, use["in", L, i, j], "x", g * GROUP + t, False)

                def down(i, part):
                    laps = 0 if part is None else part * (first["stride"] // GROUP)
                    units = PART_UNITS if i < PARTS else LAST_UNITS
                    count = units * GROUP
                    for c in range(2):
                        c0, tenants = first["down", L, i, c], use["down", L, i, c]
                        begin = count - (CLOSE_LAST if i == PARTS and c == 1 else CLOSE)
                        for j in range(count):
                            if c == 0 and j % 2 == 0:
                                need = tile["in", L, i, j // GROUP] + (j % GROUP) // 2 + 1
                                pe.wait_ge(tile_lo, need if part is None else part * stride["lo"] + need)
                            if j < begin:
                                panel_split(c0 + j, laps)
                                token_major(c0 + j, tenants, "c", j, j == 0, reg=part)
                        close_token_major(c0 + begin, laps, tenants, range(begin, count), "c")

                transposed_unit(("ln_t", L, 1), unit_panel(("in", L, 0, 0)), x,
                                arrived=lambda g: wait_normal(3 * L + 1, g))
                with pe.Fori(0, PARTS) as i:
                    for j in range(1, PART_UNITS):
                        gate_and_up(0, j, i)
                    down(0, i)
                    gate_and_up(0, 0, i + 1)
                for j in range(1, LAST_UNITS):
                    gate_and_up(PARTS, j, None)
                down(PARTS, None)


def shape_constants():
    c = np.zeros((P, C_END), np.float32)
    c[:, C_ID:C_ID + P] = np.eye(P)
    row = np.arange(P)
    for freq, sign, dim in ((C_FREQ_Q, C_SIGN_Q, HD), (C_FREQ_I, C_SIGN_I, IDX_DIM)):
        rot = dim // 4
        half = rot // 2
        inv = np.power(np.float32(ROPE_THETA), -(np.arange(half, dtype=np.float32) * np.float32(2.0) / np.float32(rot)))
        at = row % dim
        for r in range(P):
            if at[r] < rot:
                c[r, freq] = inv[at[r] % half]
                c[r, sign] = -1.0 if at[r] < half else 1.0
    c[:, C_TRI:C_TRI + P] = np.where(row[None, :] <= row[:, None], 0.0, MASKED)
    t0, s0 = row[:, None], row[None, :]
    c[:, C_ADMIT:C_ADMIT + P] = np.where(s0 // CHUNK <= t0 // CHUNK, 0.0, NOT_ADMITTED)
    s1 = np.arange(S)[None, :]
    c[:, C_ADMIT + P:C_ADMIT + P + S] = np.where(s1 // CHUNK <= (P + t0) // CHUNK, 0.0, NOT_ADMITTED)
    for g, w in enumerate(WINDOWS):
        n = np.arange(PAD) + 1
        c[:, C_INVC + g * PAD:C_INVC + (g + 1) * PAD] = np.where(n < w, w / n, 1.0)
    return c


def kernel(x, mem, positions, ev_w_in, ev_pool_w, ev_pool_scale, ev_w_out, od_w_in, od_conv_w, od_forget_b,
           od_w_out, ca_w_q, ca_w_kv, ca_w_o, ffn_w_in, ffn_w_out, ln_g, ln_b):
    import concourse.bacc as bacc
    from concourse.bass_utils import run_bass_kernel_spmd

    arrays = {n: np.ascontiguousarray(v) for n, v in dict(
        x=x, mem=mem, positions=positions, ev_w_in=ev_w_in, ev_pool_w=ev_pool_w, ev_w_out=ev_w_out,
        od_w_in=od_w_in, od_w_out=od_w_out, ca_w_q=ca_w_q, ca_w_kv=ca_w_kv, ca_w_o=ca_w_o,
        ffn_w_in=ffn_w_in, ffn_w_out=ffn_w_out, ln_g=ln_g, ln_b=ln_b).items()}
    v = np.zeros((P, V_END), np.float32)
    v[:, V_G:V_B] = np.asarray(ln_g).reshape(DEPTH * 3 * KT, P).T
    v[:, V_B:V_SCALE] = np.asarray(ln_b).reshape(DEPTH * 3 * KT, P).T
    v[:, V_SCALE:V_CONV] = np.asarray(ev_pool_scale).reshape(HALF // P, P).T
    v[:, V_CONV:V_FB] = np.asarray(od_conv_w)[0].reshape(3, HALF // P, P).transpose(2, 1, 0).reshape(P, -1)
    v[:HEADS, V_FB] = np.asarray(od_forget_b)[0]
    arrays["vectors"] = v
    arrays["shape_constants"] = shape_constants()

    nc = bacc.Bacc("TRN2", target_bir_lowering=False, num_devices=1)
    aps = {n: nc.dram_tensor(n + "_dram", v.shape, mybir.dt.from_np(v.dtype), kind="ExternalInput").ap()
           for n, v in arrays.items()}
    aps["out"] = nc.dram_tensor("out_dram", (1, S, D), F32, kind="ExternalOutput").ap()
    build(nc, aps)
    r = run_bass_kernel_spmd(nc, [{n + "_dram": v for n, v in arrays.items()}], core_ids=[0])
    return r.results[0]["out_dram"]
```
